# Optimizing a Trainium2 kernel written in Bass

```python
import math
import jax, jax.numpy as jnp
from jax import lax
import numpy as np

D_MODEL = 1024
BATCH = 1
SEQ = 256
DEPTH = 2

N_MEM = 256
D_MIX = D_MODEL
NSA_HEADS = 8
NSA_KV_HEADS = 2
NSA_GROUP = NSA_HEADS // NSA_KV_HEADS
HEAD_DIM = 64
D_NSA = NSA_HEADS * HEAD_DIM
D_KV = NSA_KV_HEADS * HEAD_DIM
ROT_DIM = HEAD_DIM // 4
ROPE_THETA = 500000.0
CMP_BLOCK = 32
CMP_STRIDE = 16
CMP_HIDDEN = 256
SEL_BLOCK = 64
SEL_TOPN = 16
WINDOW = 512
Q_BLOCK = 128
D_CONV = D_MIX // 4
CONV_WIDTH = 31
D_POOL = D_MIX // 4
POOL_WINDOWS = (2, 4, 8, 16)
POOL_GROUP = D_POOL // len(POOL_WINDOWS)
IN_SPLITS = (D_NSA,) + (D_KV,) * 6 + (3 * NSA_HEADS, D_CONV, D_CONV, D_POOL)
IN_OFFSETS = tuple(int(v) for v in np.cumsum(IN_SPLITS)[:-1])
D_IN = sum(IN_SPLITS)
XA_HEADS = 4
XA_HEAD_DIM = D_MODEL // XA_HEADS
PEER_HEADS = 8
PEER_KEYS = 128
PEER_EXPERTS = PEER_KEYS ** 2
PEER_QDIM = 256
PEER_HALF = PEER_QDIM // 2
PEER_TOPK = 16
TOKEN_CHUNK = 128
EPS = 1e-6
NEG = -1e30
FORCE = 1e4

kernel_name = 'hymba_style_nsa_conv_pool_peer_block'

def _rmsnorm(x, g):
    xf = x.astype(jnp.float32)
    y = xf * lax.rsqrt(jnp.mean(xf * xf, axis=-1, keepdims=True) + EPS)
    return (y * g.astype(jnp.float32)).astype(x.dtype)

def _layernorm(x, g, b):
    xf = x.astype(jnp.float32)
    mu = jnp.mean(xf, axis=-1, keepdims=True)
    xc = xf - mu
    y = xc * lax.rsqrt(jnp.mean(xc * xc, axis=-1, keepdims=True) + EPS)
    return (y * g.astype(jnp.float32) + b.astype(jnp.float32)).astype(x.dtype)

def _rope(x, pos):
    half = ROT_DIM // 2
    freqs = ROPE_THETA ** (-jnp.arange(half, dtype=jnp.float32) * 2.0 / ROT_DIM)
    ang = pos.astype(jnp.float32)[:, :, None, None] * freqs
    cos, sin = jnp.cos(ang), jnp.sin(ang)
    xf = x.astype(jnp.float32)
    x1, x2, rest = xf[..., :half], xf[..., half:ROT_DIM], xf[..., ROT_DIM:]
    out = jnp.concatenate([x1 * cos - x2 * sin, x1 * sin + x2 * cos, rest], axis=-1)
    return out.astype(x.dtype)

def _nsa(q, kc, vc, ks, vs, kw, vw, gates, pos, cmp_pe, cmp_w1, cmp_w2):
    B, S = q.shape[0], q.shape[1]
    scale = HEAD_DIM ** -0.5
    q, kc, ks, kw = _rope(q, pos), _rope(kc, pos), _rope(ks, pos), _rope(kw, pos)
    qg = q.reshape(B, S, NSA_KV_HEADS, NSA_GROUP, HEAD_DIM)
    tpos_all = jnp.arange(S)

    n_cmp = (S - CMP_BLOCK) // CMP_STRIDE + 1
    cidx = jnp.arange(n_cmp)[:, None] * CMP_STRIDE + jnp.arange(CMP_BLOCK)[None, :]

    def compress(t, pe, w1, w2):
        blk = t[:, cidx] + pe[None, None, :, None, :]
        blk = jnp.moveaxis(blk, 3, 2).reshape(B, n_cmp, NSA_KV_HEADS, CMP_BLOCK * HEAD_DIM)
        return jax.nn.gelu(blk @ w1) @ w2

    k_cmp = compress(kc, cmp_pe[0], cmp_w1[0], cmp_w2[0])
    v_cmp = compress(vc, cmp_pe[1], cmp_w1[1], cmp_w2[1])
    s_cmp = jnp.einsum('bskgd,bnkd->bkgsn', qg, k_cmp).astype(jnp.float32) * scale
    cmp_end = jnp.arange(n_cmp) * CMP_STRIDE + CMP_BLOCK - 1
    valid_cmp = cmp_end[None, :] <= tpos_all[:, None]
    p_cmp = jnp.where(valid_cmp, jax.nn.softmax(jnp.where(valid_cmp, s_cmp, NEG), axis=-1), 0.0)
    o_cmp = jnp.einsum('bkgsn,bnkd->bskgd', p_cmp.astype(v_cmp.dtype), v_cmp)

    n_sel = S // SEL_BLOCK
    n_top = min(SEL_TOPN, n_sel)
    ci = jnp.arange(n_cmp) * CMP_STRIDE
    sj = jnp.arange(n_sel) * SEL_BLOCK
    overlap = ((ci[:, None] < sj[None, :] + SEL_BLOCK) & (ci[:, None] + CMP_BLOCK > sj[None, :])).astype(jnp.float32)
    imp = jnp.einsum('bkgsn,nj->bksj', p_cmp, overlap)
    blk_id = jnp.arange(n_sel)[None, :]
    cur = (tpos_all // SEL_BLOCK)[:, None]
    forced = (blk_id == 0) | (blk_id == cur) | (blk_id == cur - 1)
    causal_blk = blk_id * SEL_BLOCK <= tpos_all[:, None]
    imp = jnp.where(causal_blk, jnp.where(forced, FORCE, imp), NEG)
    _, sel_idx = lax.top_k(imp, n_top)

    ks_blocks = jnp.transpose(ks.reshape(B, n_sel, SEL_BLOCK, NSA_KV_HEADS, HEAD_DIM), (0, 3, 1, 2, 4))
    vs_blocks = jnp.transpose(vs.reshape(B, n_sel, SEL_BLOCK, NSA_KV_HEADS, HEAD_DIM), (0, 3, 1, 2, 4))
    gather = jax.vmap(jax.vmap(lambda kb, ix: kb[ix]))
    kw_pad = jnp.pad(kw, ((0, 0), (WINDOW, 0), (0, 0), (0, 0)))
    vw_pad = jnp.pad(vw, ((0, 0), (WINDOW, 0), (0, 0), (0, 0)))

    def q_block(qb):
        t0 = qb * Q_BLOCK
        tpos = t0 + jnp.arange(Q_BLOCK)
        qblk = lax.dynamic_slice_in_dim(qg, t0, Q_BLOCK, axis=1)
        sidx = lax.dynamic_slice_in_dim(sel_idx, t0, Q_BLOCK, axis=2)
        kg = gather(ks_blocks, sidx)
        vg = gather(vs_blocks, sidx).reshape(B, NSA_KV_HEADS, Q_BLOCK, n_top * SEL_BLOCK, HEAD_DIM)
        kpos = sidx[..., None] * SEL_BLOCK + jnp.arange(SEL_BLOCK)
        msel = (kpos <= tpos[None, None, :, None, None]).reshape(B, NSA_KV_HEADS, 1, Q_BLOCK, n_top * SEL_BLOCK)
        s = jnp.einsum('btkgd,bktnld->bkgtnl', qblk, kg).astype(jnp.float32) * scale
        s = s.reshape(B, NSA_KV_HEADS, NSA_GROUP, Q_BLOCK, n_top * SEL_BLOCK)
        p = jax.nn.softmax(jnp.where(msel, s, NEG), axis=-1).astype(vg.dtype)
        o_sel = jnp.einsum('bkgtm,bktmd->btkgd', p, vg)
        kwb = lax.dynamic_slice_in_dim(kw_pad, t0, WINDOW + Q_BLOCK, axis=1)
        vwb = lax.dynamic_slice_in_dim(vw_pad, t0, WINDOW + Q_BLOCK, axis=1)
        kp = t0 - WINDOW + jnp.arange(WINDOW + Q_BLOCK)
        mw = (kp[None, :] >= 0) & (kp[None, :] <= tpos[:, None]) & (kp[None, :] > tpos[:, None] - WINDOW)
        sw = jnp.einsum('btkgd,bmkd->bkgtm', qblk, kwb).astype(jnp.float32) * scale
        pw = jax.nn.softmax(jnp.where(mw, sw, NEG), axis=-1).astype(vwb.dtype)
        o_win = jnp.einsum('bkgtm,bmkd->btkgd', pw, vwb)
        return o_sel, o_win

    o_sel, o_win = lax.map(q_block, jnp.arange(S // Q_BLOCK))
    o_sel = jnp.swapaxes(o_sel, 0, 1).reshape(B, S, NSA_KV_HEADS, NSA_GROUP, HEAD_DIM)
    o_win = jnp.swapaxes(o_win, 0, 1).reshape(B, S, NSA_KV_HEADS, NSA_GROUP, HEAD_DIM)
    g = jax.nn.sigmoid(gates.reshape(B, S, NSA_KV_HEADS, NSA_GROUP, 3))
    o = g[..., 0:1] * o_cmp + g[..., 1:2] * o_sel + g[..., 2:3] * o_win
    return o.reshape(B, S, D_NSA)

def _conformer_conv(a, b, conv_w, conv_b, ln_g, ln_b, pw_w, pw_b):
    h = a * jax.nn.sigmoid(b)
    h = jnp.pad(h, ((0, 0), (CONV_WIDTH - 1, 0), (0, 0)))
    h = lax.conv_general_dilated(h, conv_w[:, None, :].astype(h.dtype), window_strides=(1,), padding='VALID',
                                 dimension_numbers=('NWC', 'WIO', 'NWC'), feature_group_count=D_CONV) + conv_b
    h = jax.nn.silu(_layernorm(h, ln_g, ln_b))
    return h @ pw_w + pw_b

def _pool_mixer(h, pool_w, pool_scale):
    B, S = h.shape[0], h.shape[1]
    hf = h.astype(jnp.float32)
    c = jnp.concatenate([jnp.zeros((B, 1, D_POOL), jnp.float32), jnp.cumsum(hf, axis=1)], axis=1)
    t = jnp.arange(S)
    outs = []
    for gi, w in enumerate(POOL_WINDOWS):
        lo, hi = gi * POOL_GROUP, (gi + 1) * POOL_GROUP
        start = jnp.maximum(t + 1 - w, 0)
        cnt = (t + 1 - start).astype(jnp.float32)
        mean = (c[:, t + 1, lo:hi] - c[:, start, lo:hi]) / cnt[None, :, None]
        outs.append(mean - hf[:, :, lo:hi])
    m = jnp.stack(outs, axis=2).astype(h.dtype)
    y = jnp.einsum('bsgc,gcd->bsgd', m, pool_w).reshape(B, S, D_POOL)
    return y * pool_scale

def _cross_attention(h, memn, wq, wkv, wo):
    B, S = h.shape[0], h.shape[1]
    q = (h @ wq).reshape(B, S, XA_HEADS, XA_HEAD_DIM)
    kv = (memn @ wkv).reshape(B, memn.shape[1], 2, XA_HEADS, XA_HEAD_DIM)
    k, v = kv[:, :, 0], kv[:, :, 1]
    s = jnp.einsum('bshd,bmhd->bhsm', q, k).astype(jnp.float32) * (XA_HEAD_DIM ** -0.5)
    p = jax.nn.softmax(s, axis=-1).astype(v.dtype)
    o = jnp.einsum('bhsm,bmhd->bshd', p, v).reshape(B, S, D_MODEL)
    return o @ wo

def _peer(h, wq, sub_keys, u, v):
    B, S, D = h.shape
    T = B * S
    hf = h.reshape(T, D)
    q = (hf @ wq).reshape(T, PEER_HEADS, 2, PEER_HALF)
    s_half = jnp.einsum('thpc,pnc->thpn', q, sub_keys).astype(jnp.float32)
    v_half, i_half = lax.top_k(s_half, PEER_TOPK)
    cand = (v_half[:, :, 0, :, None] + v_half[:, :, 1, None, :]).reshape(T, PEER_HEADS, PEER_TOPK * PEER_TOPK)
    cand_idx = (i_half[:, :, 0, :, None] * PEER_KEYS + i_half[:, :, 1, None, :]).reshape(T, PEER_HEADS, PEER_TOPK * PEER_TOPK)
    top_s, top_pos = lax.top_k(cand, PEER_TOPK)
    expert_idx = jnp.take_along_axis(cand_idx, top_pos, axis=-1)
    gate = jax.nn.softmax(top_s, axis=-1).astype(h.dtype)
    n_chunks = T // TOKEN_CHUNK

    def chunk(args):
        hc, ic, gc = args
        act = jax.nn.gelu(jnp.einsum('cd,chkd->chk', hc, u[ic]))
        return jnp.einsum('chk,chkd->cd', gc * act, v[ic])

    out = lax.map(chunk, (hf.reshape(n_chunks, TOKEN_CHUNK, D),
                          expert_idx.reshape(n_chunks, TOKEN_CHUNK, PEER_HEADS, PEER_TOPK),
                          gate.reshape(n_chunks, TOKEN_CHUNK, PEER_HEADS, PEER_TOPK)))
    return out.reshape(B, S, D)

def setup_inputs(seed: int = 0) -> dict:
    key = jax.random.key(seed)
    ks = jax.random.split(key, 32)
    f32 = jnp.float32

    def nrm(k, shape, scale):
        return jax.random.normal(k, shape, f32) * scale

    def gain(k, shape):
        return 1.0 + 0.01 * jax.random.normal(k, shape, f32)

    L = DEPTH
    return {
        'x': nrm(ks[0], (BATCH, SEQ, D_MODEL), 1.0),
        'mem': nrm(ks[1], (BATCH, N_MEM, D_MODEL), 1.0),
        'positions': jax.random.randint(ks[2], (BATCH, 1), 0, 1024, jnp.int32) + jnp.arange(SEQ, dtype=jnp.int32)[None, :],
        'norm_mix_g': gain(ks[3], (L, D_MODEL)),
        'w_in': nrm(ks[4], (L, D_MODEL, D_IN), D_MODEL ** -0.5),
        'cmp_pe': nrm(ks[5], (L, 2, CMP_BLOCK, HEAD_DIM), 0.1),
        'cmp_w1': nrm(ks[6], (L, 2, CMP_BLOCK * HEAD_DIM, CMP_HIDDEN), (CMP_BLOCK * HEAD_DIM) ** -0.5),
        'cmp_w2': nrm(ks[7], (L, 2, CMP_HIDDEN, HEAD_DIM), CMP_HIDDEN ** -0.5),
        'conv_w': nrm(ks[8], (L, CONV_WIDTH, D_CONV), CONV_WIDTH ** -0.5),
        'conv_b': nrm(ks[9], (L, D_CONV), 0.01),
        'conv_ln_g': gain(ks[10], (L, D_CONV)),
        'conv_ln_b': nrm(ks[11], (L, D_CONV), 0.01),
        'conv_pw_w': nrm(ks[12], (L, D_CONV, D_CONV), D_CONV ** -0.5),
        'conv_pw_b': nrm(ks[13], (L, D_CONV), 0.01),
        'pool_w': nrm(ks[14], (L, len(POOL_WINDOWS), POOL_GROUP, POOL_GROUP), POOL_GROUP ** -0.5),
        'pool_scale': gain(ks[15], (L, D_POOL)),
        'w_out': nrm(ks[16], (L, D_MIX, D_MODEL), D_MIX ** -0.5),
        'norm_xa_g': gain(ks[17], (L, D_MODEL)),
        'norm_mem_g': gain(ks[18], (L, D_MODEL)),
        'xa_wq': nrm(ks[19], (L, D_MODEL, D_MODEL), D_MODEL ** -0.5),
        'xa_wkv': nrm(ks[20], (L, D_MODEL, 2 * D_MODEL), D_MODEL ** -0.5),
        'xa_wo': nrm(ks[21], (L, D_MODEL, D_MODEL), D_MODEL ** -0.5),
        'norm_ffn_g': gain(ks[22], (L, D_MODEL)),
        'peer_wq': nrm(ks[23], (L, D_MODEL, PEER_HEADS * PEER_QDIM), D_MODEL ** -0.5),
        'peer_subkeys': nrm(ks[24], (L, 2, PEER_KEYS, PEER_HALF), PEER_HALF ** -0.5),
        'peer_u': nrm(ks[25], (L, PEER_EXPERTS, D_MODEL), D_MODEL ** -0.5),
        'peer_v': nrm(ks[26], (L, PEER_EXPERTS, D_MODEL), PEER_HEADS ** -0.5),
        'final_g': gain(ks[27], (D_MODEL,)),
    }

def reference(x, mem, positions, norm_mix_g, w_in, cmp_pe, cmp_w1, cmp_w2, conv_w, conv_b, conv_ln_g, conv_ln_b,
              conv_pw_w, conv_pw_b, pool_w, pool_scale, w_out, norm_xa_g, norm_mem_g, xa_wq, xa_wkv, xa_wo,
              norm_ffn_g, peer_wq, peer_subkeys, peer_u, peer_v, final_g):
    B, S = x.shape[0], x.shape[1]
    for l in range(DEPTH):
        h = _rmsnorm(x, norm_mix_g[l])
        z = h @ w_in[l]
        (zq, zkc, zvc, zks, zvs, zkw, zvw, zg, za, zb, zp) = jnp.split(z, IN_OFFSETS, axis=-1)
        kv = lambda t: t.reshape(B, S, NSA_KV_HEADS, HEAD_DIM)
        o_nsa = _nsa(zq.reshape(B, S, NSA_HEADS, HEAD_DIM), kv(zkc), kv(zvc), kv(zks), kv(zvs), kv(zkw), kv(zvw),
                     zg, positions, cmp_pe[l], cmp_w1[l], cmp_w2[l])
        o_conv = _conformer_conv(za, zb, conv_w[l], conv_b[l], conv_ln_g[l], conv_ln_b[l], conv_pw_w[l], conv_pw_b[l])
        o_pool = _pool_mixer(zp, pool_w[l], pool_scale[l])
        x = x + jnp.concatenate([o_nsa, o_conv, o_pool], axis=-1) @ w_out[l]
        x = x + _cross_attention(_rmsnorm(x, norm_xa_g[l]), _rmsnorm(mem, norm_mem_g[l]), xa_wq[l], xa_wkv[l], xa_wo[l])
        x = x + _peer(_rmsnorm(x, norm_ffn_g[l]), peer_wq[l], peer_subkeys[l], peer_u[l], peer_v[l])
    return _rmsnorm(x, final_g)


_drawn_inputs = setup_inputs


def setup_inputs(seed=0):
    import zlib

    import numpy as np

    out = dict(_drawn_inputs(seed))
    spreads = {}
    factors = {'norm_mix_g': 2.745,
     'conv_ln_g': 3.11,
     'conv_ln_b': 3.285,
     'conv_pw_b': 2.788,
     'pool_scale': 2.778,
     'norm_xa_g': 5.539,
     'norm_mem_g': 4.479,
     'final_g': 38.868,
     'norm_ffn_g': 4.66}
    for name, (base, spread) in spreads.items():
        noise = np.random.default_rng([zlib.crc32(name.encode()), seed]).standard_normal(out[name].shape)
        drawn = base * np.exp(spread * noise) if base else spread * noise
        out[name] = __import__('jax').numpy.asarray(drawn.astype(out[name].dtype))
    for name, factor in factors.items():
        out[name] = (out[name] * factor).astype(out[name].dtype)
    return out
```

```python
from contextlib import ExitStack
import math

import numpy as np

import concourse.bass as bass
from concourse import mybir

F32 = mybir.dt.float32
I32 = mybir.dt.int32
U32 = mybir.dt.uint32
ALU = mybir.AluOpType
ACT = mybir.ActivationFunctionType
AX = mybir.AxisListType

P = 128
D = 1024
KC = D // P
TILES = 2
S = TILES * P
DEPTH = 2
STAGES = DEPTH * TILES
N_MEM = 256
HEADS, KV_HEADS, HD = 8, 2, 64
CMP_BLOCK, CMP_STRIDE, CMP_HIDDEN = 32, 16, 256
N_CMP = (S - CMP_BLOCK) // CMP_STRIDE + 1
NC = 16
CONV_W = 31
HIST = CONV_W - 1
POOL_WINDOWS = (2, 4, 8, 16)
XH = 4
PH, PK, TOPK = 8, 128, 16
EXPERTS = PK * PK
PAIRS = PH * TOPK
EPS = 1e-6
NEG = -1e30
LOWEST = -3.0e38
THETA, ROT = 500000.0, HD // 4
HALF = ROT // 2

B = 8
NB = PAIRS // B
BPE = 5
BDV = B - BPE
BLK = 512
RING = 2

ZC = {"q": 0, "kc": 512, "vc": 640, "ks": 768, "vs": 896, "kw": 1024, "vw": 1152, "pool": 1280}
ZW = 1536

SMALL = {}
_n = 0
for _name, _w in (("w2", 256), ("pe", 64), ("cw", 2 * CONV_W), ("cb", 2), ("lng", 2), ("lnb", 2), ("pwb", 2),
                  ("psc", 2), ("pw", 512), ("pbd", 256), ("wg", 192), ("gmix", 8), ("gxa", 8), ("gffn", 8),
                  ("subk", 256), ("first", 1)):
    SMALL[_name] = (_n, _w)
    _n += _w
N_SMALL = _n

TC = {}
_n = 0
for _name, _w in (("causal", S), ("cadd", NC), ("cvalid", NC), ("cur", 4 * P), ("prev", 4 * P), ("flag", 1)):
    TC[_name] = (_n, _w)
    _n += _w
N_TC = _n

BLOCKS = ["zq", "zk1", "zk2", "ab", "ck", "cv", "wo0", "wo1", "xq0", "xq1", "xo0", "xo1", "pq0", "pq1", "pq2", "pq3"]
MEM_BLOCKS = ["mk0", "mk1", "mv0", "mv1"]
WHERE = {n: i for i, n in enumerate(BLOCKS + MEM_BLOCKS)}

MIX_A = ["NT0", "NT1", "ZQ", "ZK1", "ZK2", "GT", "AB"]
MIX_B = ["QT", "KT", "PM", "HID", "KC"]
MIX_C = ["SC0", "SC1", "SS0", "SS1", "SS2", "SS3", "TCM", "OC"]
MIX_D = ["TS0", "TS1", "TS2", "TS3", "OS", "SW0", "SW1", "SW2", "SW3"]
MIX_E = ["TW0", "TW1", "TW2", "TW3", "OW", "CT", "CB", "PY", "PW", "OT", "WO0", "WO1"]
XATT = ["NX0", "NX1", "XQ0", "XQ1", "XS0", "XS1", "XT0", "XT1", "XO0", "XO1", "XW0", "XW1"]
ROUTE = ["NF0", "NF1", "PQ0", "PQ1", "PQ2", "PQ3", "PK0", "PK1", "PK2", "PK3"]
MEM_NORM = ["MT0", "MT1", "MT2", "MT3"]
MEM_KV = ["MK0", "MK1", "MK2", "MK3", "MV0", "MV1", "MV2", "MV3"]
LAST_USE = {"zq": "ZQ", "zk1": "ZK1", "zk2": "ZK2", "ab": "AB", "ck": "HID", "cv": "HID", "wo0": "WO0", "wo1": "WO1",
            "xq0": "XQ0", "xq1": "XQ1", "xo0": "XW0", "xo1": "XW1", "pq0": "PQ0", "pq1": "PQ1", "pq2": "PQ2",
            "pq3": "PQ3", "mk0": "MK1", "mk1": "MK3", "mv0": "MV1", "mv1": "MV3"}
BANKS = 4
TURNS = [2, 2, 1, 1, 2, 2, 2, 1, 1, 1, 1]
assert sum(TURNS) == NB

TURN_PARTS = [6.25]
for _bits in (10, 20):
    TURN_PARTS.append(round((2 * math.pi - sum(TURN_PARTS)) * 2 ** _bits) / 2 ** _bits)
TURN_PARTS.append(2 * math.pi - sum(TURN_PARTS))
ROUNDER = 1.5 * 2 ** 23

SIGNALS = [
    "tile_consts_loaded", "smalls_loaded", "fixed_loaded", "mem_loaded", "ffn_gain_loaded", "x_loaded", "out_stored",
    "vector_step", "kv_rope_done", "cmp_in_built", "h_scaled", "cmp_kv_ready", "cmp_max_taken", "cmp_probs_ready",
    "sel_scored", "win_scored", "o_mixed", "conv_out", "conv_var", "conv_normed", "conv_affine", "conv_silu",
    "x_mixed", "x_attended", "norm_var", "norm_rstd", "xs_max", "xs_probs", "experts_ranked", "mem_gained",
    "rope_reduced", "zeroed", "routed",
    "scalar_step", "x_copied", "norm_squares", "norm_std", "x_normed", "z_copied", "gate_exp", "b_exp", "q_turned",
    "k_turned", "v_kept", "pool_kept", "cmp_hidden", "cmp_exp", "cmp_turned", "sel_exp", "sel_turned", "win_exp",
    "win_turned", "pool_mean", "conv_std", "conv_exp", "cat_ready", "xq_ready", "xs_exp", "xs_turned", "xo_ready",
    "pq_ready", "pk_ready", "gate_exps", "mem_turned", "mem_kv_ready", "rope_sin", "x_kept",
    "idx_taken", "idx_staged", "gathers_issued", "h_taken", "u_free", "v_free_pe", "v_free_dv", "dots_done",
    "gelu_done", "weights_done", "diag_done", "sum_open", "sum_zeroed", "experts_added", "out_ready", "dv_added",
    "final_var", "final_std",
]


def build_program(nc, a):
    with ExitStack() as ctx:
        def sb(name, shape, dt=F32):
            return ctx.enter_context(nc.sbuf_tensor(name, shape, dt))

        def psum(name, shape):
            return ctx.enter_context(nc.psum_tensor(name, shape, F32))

        u_rows = sb("u_rows", [P, B, D])
        v_rows = sb("v_rows", [P, B, D])
        w_ring = sb("w_ring", [P, RING, KC * BLK])
        mem_k = sb("mem_k", [P, KC, N_MEM])
        mem_v = sb("mem_v", [P, 2, D])
        mem_t = sb("mem_t", [P, KC, N_MEM])
        xs = sb("xs", [P, TILES * D])
        h_t = sb("h_t", [P, KC, P])
        area1 = sb("area1", [P, 2048])
        area2 = sb("area2", [P, 2048])
        area3 = sb("area3", [P, 2048])
        kv_t = sb("kv_t", [P, 4, S + NC])
        kv_n = sb("kv_n", [P, TILES * 256])
        pool_prev = sb("pool_prev", [P, 256])
        q_t = sb("q_t", [P, 4, P])
        hid_k = sb("hid_k", [P, 2, 32])
        cmp_kt = sb("cmp_kt", [P, NC])
        cmp_vb = sb("cmp_vb", [P, HEADS, HD])
        p_cmp = sb("p_cmp", [P, HEADS, NC])
        pt_cmp = sb("pt_cmp", [P, P])
        h_ffn = sb("h_ffn", [P, D])
        hc = sb("hc", [P, 2, HIST + P])
        conv = sb("conv", [P, 2, P])
        conv_n = sb("conv_n", [P, 2, P])
        conv_e = sb("conv_e", [P, 2, P])
        smalls = sb("smalls", [P, N_SMALL])
        tcon = sb("tcon", [P, N_TC])
        acc_dv = sb("acc_dv", [P, D])
        diag = sb("diag", [P, BPE, P])
        ident = sb("ident", [P, P])
        zero = sb("zero", [P, P])
        fixed = sb("fixed", [P, HEADS + TOPK + HALF + 2 * KC])
        head_mask, iota16, freqs = fixed[:, 0:8], fixed[:, 8:24], fixed[:, 24:32]
        gain_mem = fixed[:, 32:48]
        pos = sb("pos", [P, TILES], I32)
        cos_t = sb("cos_t", [P, TILES * 20 * HALF])
        sin_t = sb("sin_t", [P, TILES * 20 * HALF])
        gates = sb("gates", [P, 24])
        st = sb("st", [P, 96])
        idx_next = sb("idx_next", [P, PAIRS], I32)
        idx = sb("idx", [P, PAIRS], I32)
        idx_batch = sb("idx_batch", [P, 2 * B], I32)
        gate_next = sb("gate_next", [P, PAIRS])
        gate = sb("gate", [P, PAIRS])
        act_b = sb("act_b", [P, B])
        gelu_b = sb("gelu_b", [P, B])
        wgt_b = sb("wgt_b", [P, B])
        half_i = sb("half_i", [P, 16, TOPK], U32)
        half_v = sb("half_v", [P, 16, TOPK])
        top_v = sb("top_v", [P, PH, TOPK])
        top_p = sb("top_p", [P, PH, TOPK], U32)

        h_ps = psum("h_ps", [P, D])
        acc_pe = psum("acc_pe", [P, D])
        bank = [psum(f"bank{i}", [P, BLK]) for i in range(BANKS)]

        x_n = area1[:, 0:D]
        probs = area1[:, :].rearrange("p (h k) -> p h k", h=HEADS)
        x_probs = area1[:, 0:XH * N_MEM].rearrange("p (h k) -> p h k", h=XH)
        half_s = area1[:, :].rearrange("p (j n) -> p j n", j=16)
        cmp_in = area2[:, 0:1024].rearrange("p (k c n) -> p k c n", k=2, c=16)
        probs_t = area2[:, :].rearrange("p (h c t) -> p h c t", h=HEADS, c=2)
        xprobs_t = area2[:, 0:1024].rearrange("p (h c t) -> p h c t", h=XH, c=2)
        mem_g = area2[:, :].rearrange("p (c m) -> p c m", c=KC)
        pq_t = area2[:, :].rearrange("p (j t) -> p j t", j=16)
        one_hot = area2[:, :].rearrange("p (h k j) -> p h k j", h=PH, k=TOPK)
        z = area3[:, 0:ZW]
        xq_t = area3[:, 0:D].rearrange("p (c t) -> p c t", c=KC)
        cand = area3[:, :].rearrange("p (h i j) -> p h i j", h=PH, i=TOPK)
        half_f = area1[:, 0:256].rearrange("p (j k) -> p j k", j=16)
        pos_f = area1[:, 256:384].rearrange("p (h k) -> p h k", h=PH)
        e_hi = area1[:, 384:512].rearrange("p (h k) -> p h k", h=PH)
        top_q = area1[:, 512:640].bitcast(U32).rearrange("p (h k) -> p h k", h=PH)
        hid_v = area2[:, 1024:1536].rearrange("p (c h n) -> p c h n", c=4, h=HEADS)
        o_sum, o_one = area3[:, 1024:1536], area3[:, 1536:2048]
        junk = area3[:, 1024:2048]
        cat_t = h_t
        rope_tmp = [area2[:, 1024 + 160 * i:1184 + 160 * i].rearrange("p (h d) -> p h d", h=20) for i in range(4)]
        xo_t = cat_t

        sems = {n: ctx.enter_context(nc.semaphore(n)) for n in SIGNALS}
        u_landed = [ctx.enter_context(nc.semaphore(f"u_landed{j}")) for j in range(B)]
        v_landed = [ctx.enter_context(nc.semaphore(f"v_landed{j}")) for j in range(B)]
        w_landed = [ctx.enter_context(nc.semaphore(f"w_landed{j}")) for j in range(RING)]
        filled = [ctx.enter_context(nc.semaphore(f"bank_filled{j}")) for j in range(BANKS)]
        drained = [ctx.enter_context(nc.semaphore(f"bank_drained{j}")) for j in range(BANKS)]
        stage_sems = [*sems.values(), *w_landed, *filled, *drained]

        def small(name, lo=0, n=None):
            at, w = SMALL[name]
            return smalls[:, at + lo:at + (w if n is None else lo + n)]

        def tile_const(name, lo=0, n=None):
            at, w = TC[name]
            return tcon[:, at + lo:at + (w if n is None else lo + n)]

        def stage(dense, experts, mem_layer=None, first=False, last=False):
            if dense is not None:
                layer, tile = dense // TILES, dense % TILES
                jobs = MIX_A + MIX_B + MIX_C + MIX_D + MIX_E + XATT
                blocks = list(BLOCKS)
                if mem_layer is not None and first:
                    jobs = MEM_NORM + MEM_KV + jobs
                    blocks = MEM_BLOCKS + blocks
                elif mem_layer is not None:
                    jobs = jobs + MEM_KV
                    blocks = blocks[:12] + MEM_BLOCKS + blocks[12:]
                jobs = jobs + ROUTE
            else:
                jobs, blocks = [], []
            at = {n: i for i, n in enumerate(jobs)}
            slot = {n: i for i, n in enumerate(blocks)}
            etile = experts % TILES if experts is not None else None

            def landed(b):
                return (experts * NB + b) * 16 + 16

            def bank_of(job):
                return bank[at[job] % BANKS]

            def wait_filled(eng, job):
                eng.wait_ge(filled[at[job] % BANKS], at[job] // BANKS + 1)

            def drain(ins, job):
                ins.then_inc(drained[at[job] % BANKS], 1)

            def weights(name):
                return w_ring[:, slot[name] % RING, :].rearrange("p (c n) -> p c n", c=KC)

            class Steps:

                def __init__(self, eng, sem):
                    self.eng, self.sem, self.n = eng, sem, 0

                def mark(self, ins):
                    ins.then_inc(self.sem, 1)
                    self.n += 1

                def settle(self, back=0):
                    if self.n - back > 0:
                        self.eng.wait_ge(self.sem, self.n - back)

                def __call__(self, ins):
                    self.mark(ins)
                    self.settle()

            with nc.Block() as block:

                @block.sync
                def _(sp):
                    if first:
                        sp.dma_start(ident[:, :], a["ident"]).then_inc(sems["fixed_loaded"], 16)
                        sp.dma_start(fixed[:, :], a["fixed"]).then_inc(sems["fixed_loaded"], 16)
                        sp.dma_start(pos[:, :], a["positions"]).then_inc(sems["fixed_loaded"], 16)
                        sp.dma_start(area1[:, :].rearrange("p (m d) -> p m d", m=2), a["mem"]).then_inc(
                            sems["mem_loaded"], 16)
                        sp.dma_start(xs[:, :].rearrange("p (t d) -> p t d", t=TILES), a["x"]).then_inc(
                            sems["x_loaded"], 16)
                    if dense is not None:
                        sp.dma_start(tcon[:, :], a["tile_consts"][bass.ds(tile, 1), :, :].rearrange(
                            "a p n -> (a p) n")).then_inc(sems["tile_consts_loaded"], 16)
                        sp.dma_start(smalls[:, :], a["smalls"][bass.ds(layer, 1), :, :].rearrange(
                            "a p n -> (a p) n")).then_inc(sems["smalls_loaded"], 16)

                    def load_gain(source):
                        if experts is not None:
                            sp.wait_ge(sems["h_taken"], 1)
                        sp.dma_start(h_ffn[:, :], source).then_inc(sems["ffn_gain_loaded"], 16)

                    for i, name in enumerate(blocks):
                        if i >= RING:
                            wait_filled(sp, LAST_USE[blocks[i - RING]])
                        src_layer = mem_layer if name in MEM_BLOCKS else layer
                        sp.dma_start(w_ring[:, i % RING, :],
                                     a["blocks"][bass.ds(src_layer * len(WHERE) + WHERE[name], 1), :, :].rearrange(
                                         "a p n -> (a p) n")).then_inc(w_landed[i % RING], 16)
                        if i == 1:
                            load_gain(a["ffn_gain"][bass.ds(layer, 1), :, :].rearrange("a p n -> (a p) n"))
                    if last:
                        load_gain(a["final_gain"])
                        for t in range(TILES):
                            sp.wait_ge(sems["out_ready"], t + 1)
                            sp.dma_start(a["out"][t * P:(t + 1) * P, :], xs[:, t * D:(t + 1) * D]).then_inc(
                                sems["out_stored"], 16)
                        sp.wait_ge(sems["out_stored"], 16 * TILES)

                @block.gpsimd
                def _(pool):
                    if experts is None:
                        return
                    nc.gpsimd.tensor_copy(idx[:, :], idx_next[:, :]).then_inc(sems["idx_taken"], 1)
                    pool.wait_ge(sems["idx_taken"], 1)
                    with pool.Fori(0, NB // 2) as b2:
                        for half in range(2):
                            nc.gpsimd.tensor_copy(idx_batch[:, half * B:(half + 1) * B],
                                                  idx[:, bass.ds(b2 * (2 * B) + half * B, B)]).then_inc(
                                                      sems["idx_staged"], 1)
                            pool.wait_ge(sems["idx_staged"], b2 * 2 + half + 1)
                            pool.sem_inc(sems["gathers_issued"], 1)
                            for j in range(B):
                                pool.wait_ge(sems["u_free"], b2 * (2 * B) + half * B + j + 1)
                                pool.sem_inc(sems["gathers_issued"], 1)
                                row = idx_batch[:, half * B + j:half * B + j + 1].bitcast(U32)
                                nc.gpsimd.indirect_dma_start(
                                    u_rows[:, j, :], None, a["u"],
                                    bass.IndirectOffsetOnAxis(ap=row, axis=0)).then_inc(u_landed[j], 16)
                            for j in range(B):
                                if j < BPE:
                                    pool.wait_ge(sems["v_free_pe"], b2 * (2 * BPE) + half * BPE + j + 1)
                                else:
                                    pool.wait_ge(sems["v_free_dv"], b2 * (2 * BDV) + half * BDV + j - BPE + 1)
                                pool.sem_inc(sems["gathers_issued"], 1)
                                row = idx_batch[:, half * B + j:half * B + j + 1].bitcast(U32)
                                nc.gpsimd.indirect_dma_start(
                                    v_rows[:, j, :], None, a["v"],
                                    bass.IndirectOffsetOnAxis(ap=row, axis=0)).then_inc(v_landed[j], 16)

                @block.vector
                def _(dve):
                    v = nc.vector
                    step = Steps(dve, sems["vector_step"])

                    def experts_start():
                        for _ in range(B):
                            dve.sem_inc(sems["u_free"], 1)
                        for _ in range(BDV):
                            dve.sem_inc(sems["v_free_dv"], 1)
                        v.tensor_copy(h_ps[:, :], h_ffn[:, :]).then_inc(sems["h_taken"], 1)
                        step.mark(v.tensor_copy(gate[:, :], gate_next[:, :]))
                        v.memset(acc_dv[:, :], 0.0).then_inc(sems["sum_zeroed"], 1)
                        dve.wait_ge(sems["h_taken"], 1)
                        dve.wait_ge(sems["sum_zeroed"], 1)
                        step.settle()

                    def expert_batches(b0, n):
                        with dve.Fori(b0, b0 + n) as b:
                            for j in range(B):
                                dve.wait_ge(u_landed[j], landed(b))
                                v.tensor_tensor_reduce(u_rows[:, j, :], u_rows[:, j, :], h_ps[:, :], 1.0, 0.0,
                                                       ALU.mult, ALU.add, act_b[:, j:j + 1]).then_inc(
                                                           sems["dots_done"], 1)
                                dve.wait_ge(sems["dots_done"], b * B + j + 1)
                                dve.sem_inc(sems["u_free"], 1)
                            dve.wait_ge(sems["gelu_done"], b + 1)
                            dve.wait_ge(sems["diag_done"], b * BPE + 1)
                            v.tensor_tensor(wgt_b[:, :], gelu_b[:, :], gate[:, bass.ds(b * B, B)],
                                            ALU.mult).then_inc(sems["weights_done"], 1)
                            dve.wait_ge(sems["weights_done"], b + 1)
                            for j in range(BPE, B):
                                dve.wait_ge(v_landed[j], landed(b))
                                v.scalar_tensor_tensor(out=acc_dv[:, :], in0=v_rows[:, j, :],
                                                       scalar=wgt_b[:, j:j + 1], in1=acc_dv[:, :],
                                                       op0=ALU.mult, op1=ALU.add).then_inc(sems["dv_added"], 1)
                                dve.wait_ge(sems["dv_added"], b * BDV + j - BPE + 1)
                                dve.sem_inc(sems["v_free_dv"], 1)

                    def experts_end():
                        rows = xs[:, bass.ds(etile * D, D)]
                        step(v.tensor_tensor(rows, rows, acc_dv[:, :], ALU.add))
                        dve.wait_ge(sems["v_free_pe"], BPE * (NB + 1))
                        v.tensor_tensor(rows, rows, acc_pe[:, :], ALU.add).then_inc(sems["experts_added"], 1)
                        dve.wait_ge(sems["experts_added"], 1)

                    norms = [0]

                    def norm_tail(n_parts=1):
                        norms[0] += 1
                        dve.wait_ge(sems["norm_squares"], norms[0])
                        v.tensor_scalar(st[:, 1:2], st[:, 0:1], 1.0 / D, EPS, ALU.mult, ALU.add).then_inc(
                            sems["norm_var"], 1)
                        dve.wait_ge(sems["norm_std"], norms[0])
                        v.reciprocal(st[:, 3:4], st[:, 2:3]).then_inc(sems["norm_rstd"], 1)

                    scaled = [0]

                    def gain_rows(jobs2, gain):
                        for i, job in enumerate(jobs2):
                            wait_filled(dve, job)
                            ins = v.tensor_tensor(
                                h_t[:, 4 * i:4 * i + 4, :], bank_of(job)[:, :].rearrange("p (c t) -> p c t", c=4),
                                small(gain, 4 * i, 4).unsqueeze(2).to_broadcast([P, 4, P]), ALU.mult)
                            drain(ins, job)

                    def rope_tables():
                        pf = st[:, 64:66]
                        ang, tmp, turns = st[:, 8:24], st[:, 24:40], st[:, 40:56]
                        dve.wait_ge(sems["fixed_loaded"], 48)
                        step(v.tensor_copy(pf, pos[:, :]))
                        for t in range(TILES):
                            step(v.tensor_scalar(ang[:, 8 * t:8 * t + 8], freqs, pf[:, t:t + 1], None, ALU.mult))
                        for scale in (4096.0, 1.0):
                            step(v.tensor_scalar(turns, ang, 1.0 / (2 * math.pi * scale), None, ALU.mult))
                            step(v.tensor_scalar(turns, turns, ROUNDER, ROUNDER, ALU.add, ALU.subtract))
                            for part in TURN_PARTS:
                                step(v.scalar_tensor_tensor(out=ang, in0=turns, scalar=-part * scale, in1=ang,
                                                            op0=ALU.mult, op1=ALU.add))
                        step(v.tensor_scalar(tmp, ang, math.pi / 2, -2 * math.pi, ALU.is_gt, ALU.mult))
                        step(v.scalar_tensor_tensor(out=tmp, in0=ang, scalar=math.pi / 2, in1=tmp,
                                                    op0=ALU.add, op1=ALU.add))
                        lim = 3.1415925
                        step(v.tensor_scalar(tmp, tmp, lim, -lim, ALU.min, ALU.max))
                        step(v.tensor_scalar(ang, ang, lim, -lim, ALU.min, ALU.max))
                        step(v.memset(cos_t[:, :], 1.0))
                        v.memset(sin_t[:, :], 0.0).then_inc(sems["rope_reduced"], 1)
                        dve.wait_ge(sems["rope_sin"], 2)
                        for t in range(TILES):
                            for table, src in ((cos_t, tmp), (sin_t, ang)):
                                heads = table[:, t * 160:(t + 1) * 160].rearrange("p (h d) -> p h d", h=20)
                                for lo, n in ((0, 10), (12, 2), (16, 2)):
                                    step.mark(v.tensor_copy(
                                        heads[:, lo:lo + n, :],
                                        src[:, 8 * t:8 * t + 8].unsqueeze(1).to_broadcast([P, n, HALF])))
                        step.settle()

                    def mem_gain():
                        if not first:
                            wait_filled(dve, "XO1")
                        else:
                            dve.wait_ge(sems["mem_turned"], 4)
                        v.tensor_tensor(mem_g, mem_t[:, :, :],
                                        gain_mem[:, mem_layer * KC:(mem_layer + 1) * KC].unsqueeze(2).to_broadcast(
                                            [P, KC, N_MEM]), ALU.mult).then_inc(sems["mem_gained"], 1)

                    def part0():
                        if first:
                            step.mark(v.memset(kv_t[:, :, :], 0.0))
                            step.mark(v.memset(kv_n[:, :], 0.0))
                            step.mark(v.memset(hc[:, :, :], 0.0))
                            step.mark(v.memset(pool_prev[:, :], 0.0))
                            v.memset(zero[:, :], 0.0).then_inc(sems["zeroed"], 1)
                            rope_tables()
                            norm_tail()
                            norm_tail()
                            mem_gain()
                        norm_tail()
                        dve.wait_ge(sems["smalls_loaded"], 16)
                        dve.wait_ge(sems["tile_consts_loaded"], 16)
                        gain_rows(["NT0", "NT1"], "gmix")
                        step(v.tensor_scalar(hc[:, :, 0:HIST], hc[:, :, P:P + HIST], tile_const("flag"), None, ALU.mult))
                        dve.wait_ge(sems["z_copied"], 3)
                        turn = [z[:, 0:1280].rearrange("p (h d) -> p h d", h=20)[:, :, i * HALF:(i + 1) * HALF]
                                for i in range(2)]
                        c = cos_t[:, bass.ds(tile * 160, 160)].rearrange("p (h d) -> p h d", h=20)
                        s = sin_t[:, bass.ds(tile * 160, 160)].rearrange("p (h d) -> p h d", h=20)
                        for tmp, (i, table) in zip(rope_tmp, ((0, c), (1, s), (0, s), (1, c))):
                            step.mark(v.tensor_tensor(tmp, turn[i], table, ALU.mult))
                        step.settle()
                        step.mark(v.tensor_tensor(turn[0], rope_tmp[0], rope_tmp[1], ALU.subtract))
                        v.tensor_tensor(turn[1], rope_tmp[2], rope_tmp[3], ALU.add).then_inc(sems["kv_rope_done"], 1)
                        step.settle()
                        dve.wait_ge(sems["gate_exp"], 1)
                        step(v.tensor_scalar(gates[:, :], gates[:, :], 1.0, None, ALU.add))
                        step(v.reciprocal(gates[:, :], gates[:, :]))
                        dve.wait_ge(sems["b_exp"], 1)
                        step(v.tensor_scalar(conv_e[:, :, :], conv_e[:, :, :], 1.0, None, ALU.add))
                        step(v.reciprocal(conv_e[:, :, :], conv_e[:, :, :]))
                        ins = v.tensor_tensor(hc[:, :, HIST:HIST + P],
                                              bank_of("AB")[:, 0:256].rearrange("p (g t) -> p g t", g=2),
                                              conv_e[:, :, :], ALU.mult)
                        drain(ins, "AB")
                        dve.wait_ge(drained[at["AB"] % BANKS], at["AB"] // BANKS + 1)

                    def part1():
                        dve.wait_ge(sems["k_turned"], 1)
                        for kind in range(2):
                            for kvh in range(KV_HEADS):
                                rows = slice(kvh * HD, (kvh + 1) * HD)
                                for half in range(2):
                                    out = cmp_in[half * HD:(half + 1) * HD, kind, :, kvh * NC:(kvh + 1) * NC]
                                    src = kv_t[rows, kind, 0:S].rearrange("p (n r) -> p n r", r=CMP_STRIDE)
                                    at_pe, _ = SMALL["pe"]
                                    for hi in range(2):
                                        tok = kv_t[rows, kind, hi * CMP_STRIDE:hi * CMP_STRIDE + S].rearrange(
                                            "p (n c e) -> p c n e", c=8, e=2)[:, :, :, half]
                                        pe_c = smalls[rows, at_pe + kind * 32 + half * 16 + hi * 8:
                                                      at_pe + kind * 32 + half * 16 + hi * 8 + 8]
                                        ins = v.tensor_tensor(out[:, hi * 8:hi * 8 + 8, :], tok,
                                                              pe_c.unsqueeze(2).to_broadcast([HD, 8, NC]), ALU.add)
                                        ins.then_inc(sems["cmp_in_built"], 1)
                        for g in range(2):
                            step.mark(v.tensor_scalar(conv[:, g, :], hc[:, g, 0:P], small("cw", g * CONV_W, 1),
                                                      small("cb", g, 1), ALU.mult, ALU.add))
                        for k in range(1, CONV_W):
                            for g in range(2):
                                step.settle(1)
                                ins = v.scalar_tensor_tensor(out=conv[:, g, :], in0=hc[:, g, k:k + P],
                                                             scalar=small("cw", g * CONV_W + k, 1), in1=conv[:, g, :],
                                                             op0=ALU.mult, op1=ALU.add)
                                if k == CONV_W - 1:
                                    ins.then_inc(sems["conv_out"], 1)
                                else:
                                    step.mark(ins)
                                if k == CONV_W - 1 and g == 0:
                                    step.settle()
                        dve.wait_ge(sems["conv_out"], 2)
                        wait_filled(dve, "KC")
                        step(v.tensor_copy(cmp_kt[:, :], bank_of("KC")[:, 0:NC]))
                        ins = v.tensor_tensor(
                            cmp_vb[:, :, :].rearrange("p (k g) d -> p k g d", k=KV_HEADS),
                            bank_of("KC")[:, NC:NC + P].rearrange("p (k d) -> p k d", k=KV_HEADS).unsqueeze(2)
                            .to_broadcast([P, KV_HEADS, 4, HD]),
                            head_mask.rearrange("p (k g) -> p k g", k=KV_HEADS).unsqueeze(3).to_broadcast(
                                [P, KV_HEADS, 4, HD]), ALU.mult)
                        drain(ins, "KC")

                    def score_pairs(prefix, signal):
                        for i in range(4):
                            job = f"{prefix}{i}"
                            h0 = (i % 2) * 4 + 2 * (i // 2)
                            wait_filled(dve, job)
                            ins = v.scalar_tensor_tensor(
                                out=probs[:, h0:h0 + 2, :], in0=bank_of(job)[:, :].rearrange("p (h k) -> p h k", h=2),
                                scalar=HD ** -0.5, in1=tile_const("causal").unsqueeze(1).to_broadcast([P, 2, S]),
                                op0=ALU.mult, op1=ALU.add)
                            drain(ins, job)
                            dve.wait_ge(drained[at[job] % BANKS], at[job] // BANKS + 1)
                            v.tensor_reduce(st[:, 8 + h0:8 + h0 + 2], probs[:, h0:h0 + 2, :], AX.X, ALU.max,
                                            negate=True).then_inc(sems[signal], 1)

                    def gated(branch, sums):
                        co = st[:, 32:40]
                        step(v.reciprocal(co, sums))
                        step(v.tensor_tensor(co, co, gates[:, :].rearrange("p (h b) -> p h b", b=3)[:, :, branch],
                                             ALU.mult))
                        return co.unsqueeze(2).to_broadcast([P, HEADS, HD])

                    def heads_of(t):
                        return t.rearrange("p (h d) -> p h d", h=HEADS)

                    def part2():
                        for i in range(2):
                            job = f"SC{i}"
                            wait_filled(dve, job)
                            ins = v.scalar_tensor_tensor(
                                out=p_cmp[:, 4 * i:4 * i + 4, :],
                                in0=bank_of(job)[:, 0:4 * NC].rearrange("p (h n) -> p h n", h=4),
                                scalar=HD ** -0.5, in1=tile_const("cadd").unsqueeze(1).to_broadcast([P, 4, NC]),
                                op0=ALU.mult, op1=ALU.add)
                            drain(ins, job)
                            dve.wait_ge(drained[at[job] % BANKS], at[job] // BANKS + 1)
                        step(v.tensor_reduce(st[:, 16:24], p_cmp[:, :, :], AX.X, ALU.max, negate=True))
                        v.tensor_tensor(p_cmp[:, :, :], p_cmp[:, :, :],
                                        st[:, 16:24].unsqueeze(2).to_broadcast([P, HEADS, NC]), ALU.add).then_inc(
                                            sems["cmp_max_taken"], 1)
                        score_pairs("SS", "sel_scored")
                        dve.wait_ge(sems["cmp_exp"], 1)
                        step(v.tensor_reduce(st[:, 24:32], p_cmp[:, :, :], AX.X, ALU.add))
                        v.tensor_tensor(p_cmp[:, :, :], p_cmp[:, :, :],
                                        tile_const("cvalid").unsqueeze(1).to_broadcast([P, HEADS, NC]),
                                        ALU.mult).then_inc(sems["cmp_probs_ready"], 1)
                        co = gated(0, st[:, 24:32])
                        wait_filled(dve, "OC")
                        ins = v.tensor_tensor(heads_of(o_sum), heads_of(bank_of("OC")[:, :]), co, ALU.mult)
                        drain(ins, "OC")
                        dve.wait_ge(drained[at["OC"] % BANKS], at["OC"] // BANKS + 1)

                    def add_branch(job, branch, sums):
                        co = gated(branch, sums)
                        wait_filled(dve, job)
                        ins = v.tensor_tensor(heads_of(o_one), heads_of(bank_of(job)[:, :]), co, ALU.mult)
                        drain(ins, job)
                        dve.wait_ge(drained[at[job] % BANKS], at[job] // BANKS + 1)
                        return v.tensor_tensor(o_sum, o_sum, o_one, ALU.add)

                    def part3():
                        dve.wait_ge(sems["sel_exp"], HEADS)
                        step(add_branch("OS", 1, st[:, 40:48]))
                        wait_filled(dve, "TS3")
                        score_pairs("SW", "win_scored")

                    def part4():
                        dve.wait_ge(sems["win_exp"], HEADS)
                        add_branch("OW", 2, st[:, 48:56]).then_inc(sems["o_mixed"], 1)
                        wait_filled(dve, "CT")
                        ct = bank_of("CT")[:, 0:256]
                        step(v.bn_stats(st[:, 64:70], ct))
                        step(v.bn_aggr(st[:, 70:72], st[:, 64:70]))
                        v.tensor_scalar(st[:, 72:73], st[:, 71:72], EPS, None, ALU.add).then_inc(sems["conv_var"], 1)
                        dve.wait_ge(sems["conv_std"], 1)
                        step(v.reciprocal(st[:, 74:75], st[:, 73:74]))
                        ins = v.tensor_scalar(conv_n[:, :, :].rearrange("p g t -> p (g t)"), ct, st[:, 70:71],
                                              st[:, 74:75], ALU.subtract, ALU.mult)
                        drain(ins, "CT")
                        wait_filled(dve, "CB")
                        for g in range(2):
                            ins = v.tensor_scalar(conv[:, g, :], bank_of("CB")[:, g * P:(g + 1) * P],
                                                  small("lng", g, 1), small("lnb", g, 1), ALU.mult, ALU.add)
                            if g == 0:
                                step.mark(ins)
                            else:
                                drain(ins, "CB")
                        step.settle()
                        dve.wait_ge(drained[at["CB"] % BANKS], at["CB"] // BANKS + 1)
                        dve.sem_inc(sems["conv_affine"], 1)
                        dve.wait_ge(sems["conv_exp"], 1)
                        step(v.tensor_scalar(conv_e[:, :, :], conv_e[:, :, :], 1.0, None, ALU.add))
                        step(v.reciprocal(conv_e[:, :, :], conv_e[:, :, :]))
                        v.tensor_tensor(conv_n[:, :, :], conv[:, :, :], conv_e[:, :, :], ALU.mult).then_inc(
                            sems["conv_silu"], 1)
                        add_to_x(["WO0", "WO1"], "x_mixed")

                    def add_to_x(jobs2, signal):
                        for i, job in enumerate(jobs2):
                            cols = xs[:, bass.ds(tile * D + i * BLK, BLK)]
                            wait_filled(dve, job)
                            ins = v.tensor_tensor(cols, cols, bank_of(job)[:, :], ALU.add)
                            drain(ins, job)
                        for job in jobs2:
                            dve.wait_ge(drained[at[job] % BANKS], at[job] // BANKS + 1)
                        dve.sem_inc(sems[signal], 1)

                    def part5():
                        norm_tail()
                        gain_rows(["NX0", "NX1"], "gxa")
                        for i in range(2):
                            job = f"XS{i}"
                            wait_filled(dve, job)
                            step(v.tensor_reduce(st[:, 8 + 2 * i:10 + 2 * i],
                                                 bank_of(job)[:, :].rearrange("p (h k) -> p h k", h=2), AX.X, ALU.max,
                                                 negate=True))
                            v.tensor_scalar(st[:, 16 + 2 * i:18 + 2 * i], st[:, 8 + 2 * i:10 + 2 * i],
                                            (D // XH) ** -0.5, None, ALU.mult).then_inc(sems["xs_max"], 1)
                        dve.wait_ge(sems["xs_exp"], XH)
                        step(v.reciprocal(st[:, 24:28], st[:, 20:24]))
                        v.tensor_tensor(x_probs, x_probs, st[:, 24:28].unsqueeze(2).to_broadcast([P, XH, N_MEM]),
                                        ALU.mult).then_inc(sems["xs_probs"], 1)
                        add_to_x(["XW0", "XW1"], "x_attended")
                        if mem_layer is not None and not first:
                            mem_gain()

                    def part6():
                        norm_tail()
                        dve.wait_ge(sems["ffn_gain_loaded"], 16)
                        dve.wait_ge(sems["x_normed"], norms[0])
                        step(v.tensor_tensor(h_ffn[:, :], x_n, h_ffn[:, :], ALU.mult))
                        gain_rows(["NF0", "NF1"], "gffn")

                    def top16(values, top, where, groups):
                        for g in groups:
                            step.mark(v.max(top[:, g, 0:8], values(g)))
                        step.settle()
                        for g in groups:
                            step.mark(v.max_index(where[:, g, 0:8], top[:, g, 0:8], values(g)))
                        step.settle()
                        for g in groups:
                            step.mark(v.match_replace(values(g), top[:, g, 0:8], values(g), LOWEST))
                        step.settle()
                        for g in groups:
                            step.mark(v.max(top[:, g, 8:16], values(g)))
                        step.settle()
                        for g in groups:
                            step.mark(v.max_index(where[:, g, 8:16], top[:, g, 8:16], values(g)))
                        step.settle()

                    def part7(quarter):
                        dve.wait_ge(sems["pk_ready"], 2 * quarter + 2)
                        top16(lambda g: half_s[:, g, :], half_v, half_i, range(8 * quarter, 8 * quarter + 8))

                    def part8():
                        pairs = half_v[:, :, :].rearrange("p (h e) k -> p h e k", e=2)
                        shape = [P, PH, TOPK, TOPK]
                        step(v.tensor_tensor(cand, pairs[:, :, 0, :].unsqueeze(3).to_broadcast(shape),
                                             pairs[:, :, 1, :].unsqueeze(2).to_broadcast(shape), ALU.add))
                        step(v.tensor_copy(half_f, half_i[:, :, :]))
                        top16(lambda g: cand[:, g, :, :].rearrange("p i j -> p (i j)"), top_v, top_p, range(PH))
                        if experts is not None:
                            dve.wait_ge(sems["idx_taken"], 1)
                        step(v.tensor_tensor(gate_next[:, :].rearrange("p (h k) -> p h k", h=PH), top_v[:, :, :],
                                             top_v[:, :, 0:1].to_broadcast([P, PH, TOPK]), ALU.subtract))
                        dve.sem_inc(sems["experts_ranked"], 1)

                    def part9():
                        halves = half_f.rearrange("p (h e) k -> p h e k", e=2)
                        shape = [P, PH, TOPK, TOPK]
                        for e, (op, by) in enumerate(((ALU.logical_shift_right, 4), (ALU.bitwise_and, 15))):
                            step(v.tensor_scalar(top_q, top_p[:, :, :], by, None, op))
                            step(v.tensor_copy(pos_f, top_q))
                            step(v.tensor_tensor(one_hot, pos_f.unsqueeze(3).to_broadcast(shape),
                                                 iota16.unsqueeze(1).unsqueeze(1).to_broadcast(shape), ALU.is_equal))
                            step(v.tensor_tensor(one_hot, one_hot, halves[:, :, e, :].unsqueeze(2).to_broadcast(shape),
                                                 ALU.mult))
                            if e == 0:
                                step(v.tensor_reduce(e_hi, one_hot, AX.X, ALU.add))
                                step(v.tensor_scalar(e_hi, e_hi, float(PK), small("first"),
                                                     ALU.mult, ALU.add))
                            else:
                                step(v.tensor_reduce(pos_f, one_hot, AX.X, ALU.add))
                        step(v.tensor_tensor(idx_next[:, :].rearrange("p (h k) -> p h k", h=PH), e_hi,
                                             pos_f, ALU.add))
                        dve.wait_ge(sems["gate_exps"], 1)
                        g3 = gate_next[:, :].rearrange("p (h k) -> p h k", h=PH)
                        step(v.tensor_reduce(st[:, 8:16], g3, AX.X, ALU.add))
                        step(v.reciprocal(st[:, 16:24], st[:, 8:16]))
                        step(v.tensor_tensor(g3, g3, st[:, 16:24].unsqueeze(2).to_broadcast([P, PH, TOPK]), ALU.mult))

                    if experts is not None:
                        experts_start()
                    if dense is not None:
                        parts = [part0, part1, part2, part3, part4, part5, part6, lambda: part7(0),
                                 lambda: part7(1), part8, part9]
                        b0 = 0
                        for part, n in zip(parts, TURNS):
                            part()
                            if experts is not None:
                                expert_batches(b0, n)
                            b0 += n
                    else:
                        expert_batches(0, NB)
                    if experts is not None:
                        experts_end()
                    if last:
                        dve.wait_ge(sems["ffn_gain_loaded"], 16)
                        for t in range(TILES):
                            rows = xs[:, t * D:(t + 1) * D]
                            dve.wait_ge(sems["norm_squares"], t + 1)
                            v.tensor_scalar(st[:, 1:2], st[:, 0:1], 1.0 / D, EPS, ALU.mult, ALU.add).then_inc(
                                sems["final_var"], 1)
                            dve.wait_ge(sems["final_std"], t + 1)
                            step(v.reciprocal(st[:, 3:4], st[:, 2:3]))
                            v.scalar_tensor_tensor(out=rows, in0=rows, scalar=st[:, 3:4], in1=h_ffn[:, :],
                                                   op0=ALU.mult, op1=ALU.mult).then_inc(sems["out_ready"], 1)
                            dve.wait_ge(sems["out_ready"], t + 1)

                @block.scalar
                def _(act):
                    s = nc.scalar
                    step = Steps(act, sems["scalar_step"])

                    def expert_batches(b0, n):
                        with act.Fori(b0, b0 + n) as b:
                            act.wait_ge(sems["dots_done"], b * B + B)
                            s.activation(gelu_b[:, :], act_b[:, :], ACT.Gelu_apprx_tanh).then_inc(
                                sems["gelu_done"], 1)
                            act.wait_ge(sems["weights_done"], b + 1)
                            for j in range(BPE):
                                act.wait_ge(sems["v_free_pe"], b * BPE + j + 1)
                                s.activation(diag[:, j, :], ident[:, :], ACT.Copy,
                                             scale=wgt_b[:, j:j + 1]).then_inc(sems["diag_done"], 1)

                    norms = [0]

                    def norm(src, squares, wait_x=None):
                        norms[0] += 1
                        s.activation(squares, src, ACT.Square, accum_out=st[:, 0:1]).then_inc(sems["norm_squares"], 1)
                        act.wait_ge(sems["norm_var"], norms[0])
                        s.activation(st[:, 2:3], st[:, 1:2], ACT.Sqrt).then_inc(sems["norm_std"], 1)
                        act.wait_ge(sems["norm_rstd"], norms[0])
                        return s.activation(x_n, src, ACT.Copy, scale=st[:, 3:4])

                    def copy_bank(out, job, signal=None, func=ACT.Copy, cols=None, view=None, **kw):
                        wait_filled(act, job)
                        src = bank_of(job)[:, 0:cols] if cols else bank_of(job)[:, :]
                        if view:
                            src = view(src)
                        drain(s.activation(out, src, func, **kw), job)
                        if signal:
                            act.wait_ge(drained[at[job] % BANKS], at[job] // BANKS + 1)
                            act.sem_inc(sems[signal], 1)

                    def c_t(n):
                        return lambda ap: ap.rearrange("p (c t) -> p c t", c=n)

                    def mem_kv():
                        for i in range(4):
                            copy_bank(mem_k[:, 2 * i:2 * i + 2, :], f"MK{i}", "mem_kv_ready", view=c_t(2))
                        for i in range(4):
                            copy_bank(mem_v[:, i % 2, (i // 2) * BLK:(i // 2 + 1) * BLK], f"MV{i}", "mem_kv_ready")

                    def part0():
                        if first:
                            act.wait_ge(sems["rope_reduced"], 1)
                            s.activation(st[:, 24:40], st[:, 24:40], ACT.Sin).then_inc(sems["rope_sin"], 1)
                            s.activation(st[:, 8:24], st[:, 8:24], ACT.Sin).then_inc(sems["rope_sin"], 1)
                            act.wait_ge(sems["mem_loaded"], 16)
                            for m in range(2):
                                src = area1[:, m * D:(m + 1) * D]
                                norms[0] += 1
                                s.activation(junk, src, ACT.Square, accum_out=st[:, 0:1]).then_inc(
                                    sems["norm_squares"], 1)
                                act.wait_ge(sems["norm_var"], norms[0])
                                s.activation(st[:, 2:3], st[:, 1:2], ACT.Sqrt).then_inc(sems["norm_std"], 1)
                                act.wait_ge(sems["norm_rstd"], norms[0])
                                s.activation(src, src, ACT.Copy, scale=st[:, 3:4]).then_inc(sems["x_normed"], 1)
                            for i in range(4):
                                copy_bank(mem_t[:, (i % 2) * 4:(i % 2) * 4 + 4, (i // 2) * P:(i // 2 + 1) * P],
                                          f"MT{i}", "mem_turned", view=c_t(4))
                            mem_kv()
                            act.wait_ge(sems["x_loaded"], 16)
                        norm(xs[:, bass.ds(tile * D, D)], junk).then_inc(sems["x_normed"], 1)
                        copy_bank(z[:, 0:512], "ZQ", "z_copied")
                        copy_bank(z[:, 512:1024], "ZK1", "z_copied")
                        copy_bank(z[:, 1024:1536], "ZK2", "z_copied")
                        copy_bank(gates[:, :], "GT", "gate_exp", func=ACT.Exp, cols=24, scale=-1.0)
                        wait_filled(act, "AB")
                        s.activation(conv_e[:, :, :], bank_of("AB")[:, 256:512].rearrange("p (g t) -> p g t", g=2),
                                     ACT.Exp, scale=-1.0).then_inc(sems["b_exp"], 1)

                    def part1():
                        copy_bank(q_t[:, :, :], "QT", "q_turned", view=c_t(4))
                        copy_bank(kv_t[:, :, bass.ds(tile * P, P)], "KT", "k_turned", view=c_t(4))
                        act.wait_ge(sems["kv_rope_done"], 1)
                        s.activation(kv_n[:, bass.ds(tile * 256, 256)].rearrange("p (k d) -> p k d", k=2),
                                     z[:, ZC["vs"]:ZC["vs"] + 512].rearrange("p (k d) -> p k d", k=2)[:, :, 0:P],
                                     ACT.Copy).then_inc(sems["v_kept"], 1)
                        copy_bank(pool_m[:, :, :], "PM", "pool_mean", cols=256, view=c_t(2))
                        s.activation(pool_prev[:, :], z[:, ZC["pool"]:ZC["pool"] + 256], ACT.Copy).then_inc(
                            sems["pool_kept"], 1)
                        wait_filled(act, "HID")
                        hid = bank_of("HID")
                        s.activation(hid_k[:, :, :], hid[:, 0:64].rearrange("p (c n) -> p c n", c=2),
                                     ACT.Gelu_apprx_tanh).then_inc(sems["cmp_hidden"], 1)
                        ins = s.activation(hid_v,
                                           hid[:, 64:128].rearrange("p (c n) -> p c n", c=4).unsqueeze(2).to_broadcast(
                                               [P, 4, HEADS, NC]), ACT.Gelu_apprx_tanh)
                        drain(ins, "HID")

                    def exp_heads(scored, done, col):
                        for i in range(4):
                            act.wait_ge(sems[scored], i + 1)
                            for k in range(2):
                                h = (i % 2) * 4 + 2 * (i // 2) + k
                                s.activation(probs[:, h, :], probs[:, h, :], ACT.Exp, bias=st[:, 8 + h:9 + h],
                                             accum_out=st[:, col + h:col + h + 1]).then_inc(sems[done], 1)

                    def part2():
                        act.wait_ge(sems["cmp_max_taken"], 1)
                        s.activation(p_cmp[:, :, :], p_cmp[:, :, :], ACT.Exp).then_inc(sems["cmp_exp"], 1)
                        exp_heads("sel_scored", "sel_exp", 40)
                        copy_bank(pt_cmp[:, :], "TCM", "cmp_turned", cols=P)

                    def turn_probs(prefix, signal):
                        for i in range(4):
                            copy_bank(probs_t[:, 2 * i:2 * i + 2, :, :].rearrange("p h c t -> p (h c) t"),
                                      f"{prefix}{i}", signal, view=c_t(4))

                    def part3():
                        turn_probs("TS", "sel_turned")
                        exp_heads("win_scored", "win_exp", 48)

                    def part4():
                        wait_filled(act, "OS")
                        turn_probs("TW", "win_turned")
                        act.wait_ge(sems["conv_var"], 1)
                        s.activation(st[:, 73:74], st[:, 72:73], ACT.Sqrt).then_inc(sems["conv_std"], 1)
                        act.wait_ge(sems["conv_affine"], 1)
                        s.activation(conv_e[:, :, :], conv[:, :, :], ACT.Exp, scale=-1.0).then_inc(sems["conv_exp"], 1)
                        wait_filled(act, "PY")
                        for i in range(2):
                            ins = s.activation(cat_t[:, 6 + i, :], bank_of("PY")[:, i * P:(i + 1) * P], ACT.Copy,
                                               scale=small("psc", i, 1))
                            if i == 0:
                                step.mark(ins)
                            else:
                                drain(ins, "PY")
                        wait_filled(act, "PW")
                        for i in range(2):
                            ins = s.activation(cat_t[:, 4 + i, :], bank_of("PW")[:, i * P:(i + 1) * P], ACT.Identity,
                                               bias=small("pwb", i, 1))
                            if i == 0:
                                step.mark(ins)
                            else:
                                drain(ins, "PW")
                        step.settle()
                        for job in ("PY", "PW"):
                            act.wait_ge(drained[at[job] % BANKS], at[job] // BANKS + 1)
                        copy_bank(cat_t[:, 0:4, :], "OT", "cat_ready", view=c_t(4))

                    def part5():
                        act.wait_ge(sems["x_mixed"], 1)
                        norm(xs[:, bass.ds(tile * D, D)], junk).then_inc(sems["x_normed"], 1)
                        for i in range(2):
                            copy_bank(xq_t[:, 4 * i:4 * i + 4, :], f"XQ{i}", "xq_ready", view=c_t(4))
                        for i in range(2):
                            act.wait_ge(sems["xs_max"], i + 1)
                            for k in range(2):
                                h = 2 * i + k
                                ins = s.activation(x_probs[:, h, :], bank_of(f"XS{i}")[:, k * N_MEM:(k + 1) * N_MEM],
                                                   ACT.Exp, bias=st[:, 16 + h:17 + h], scale=(D // XH) ** -0.5,
                                                   accum_out=st[:, 20 + h:21 + h])
                                if k == 0:
                                    ins.then_inc(sems["xs_exp"], 1)
                                else:
                                    drain(ins, f"XS{i}")
                                    act.wait_ge(drained[at[f"XS{i}"] % BANKS], at[f"XS{i}"] // BANKS + 1)
                                    act.sem_inc(sems["xs_exp"], 1)
                        for i in range(2):
                            copy_bank(xprobs_t[:, 2 * i:2 * i + 2, :, :].rearrange("p h c t -> p (h c) t"), f"XT{i}",
                                      "xs_turned", view=c_t(4))
                        for i in range(2):
                            copy_bank(xo_t[:, 4 * i:4 * i + 4, :], f"XO{i}", "xo_ready", view=c_t(4))
                        act.wait_ge(sems["x_attended"], 1)
                        if mem_layer is not None and not first:
                            mem_kv()

                    def part6():
                        norm(xs[:, bass.ds(tile * D, D)], junk).then_inc(sems["x_normed"], 1)
                        for i in range(4):
                            copy_bank(pq_t[:, 4 * i:4 * i + 4, :], f"PQ{i}", "pq_ready", view=c_t(4))
                        dve_done = norms[0]
                        wait_filled(act, "NF1")
                        for i in range(4):
                            copy_bank(half_s[:, 4 * i:4 * i + 4, :], f"PK{i}", "pk_ready", view=c_t(4))

                    def part9():
                        act.wait_ge(sems["experts_ranked"], 1)
                        s.activation(gate_next[:, :], gate_next[:, :], ACT.Exp).then_inc(sems["gate_exps"], 1)

                    def nothing():
                        pass

                    if last:
                        s.activation(junk, xs[:, 0:D], ACT.Square, accum_out=st[:, 0:1]).then_inc(
                            sems["norm_squares"], 1)
                    if dense is not None:
                        parts = [part0, part1, part2, part3, part4, part5, part6, nothing, nothing, nothing, part9]
                        b0 = 0
                        for part, n in zip(parts, TURNS):
                            part()
                            if experts is not None:
                                expert_batches(b0, n)
                            b0 += n
                    else:
                        expert_batches(0, NB)
                    if last:
                        for t in range(TILES):
                            if t == 1:
                                act.wait_ge(sems["experts_added"], 1)
                                act.wait_ge(sems["out_ready"], 1)
                                s.activation(junk, xs[:, D:2 * D], ACT.Square, accum_out=st[:, 0:1]).then_inc(
                                    sems["norm_squares"], 1)
                            act.wait_ge(sems["final_var"], t + 1)
                            s.activation(st[:, 2:3], st[:, 1:2], ACT.Sqrt).then_inc(sems["final_std"], 1)

                @block.tensor
                def _(pe):
                    def expert_batches(b0, n):
                        with pe.Fori(b0, b0 + n) as b:
                            for j in range(BPE):
                                pe.wait_ge(v_landed[j], landed(b))
                                pe.wait_ge(sems["diag_done"], BPE + b * BPE + j + 1)
                                for c in range(2):
                                    mm = pe.matmul(acc_pe[:, c * 512:(c + 1) * 512], diag[:, j, :],
                                                   v_rows[:, j, c * 512:(c + 1) * 512], start=False, stop=False,
                                                   skip_group_check=True)
                                mm.then_inc(sems["v_free_pe"], 1)

                    def open_job(job):
                        if at[job] >= BANKS:
                            pe.wait_ge(drained[at[job] % BANKS], at[job] // BANKS)
                        return bank_of(job)

                    def close_job(mm, job):
                        mm.then_inc(filled[at[job] % BANKS], 1)

                    def need_weights(name):
                        pe.wait_ge(w_landed[slot[name] % RING], 16 * (slot[name] // RING + 1))
                        return weights(name)

                    def turn(job, sources):
                        out = open_job(job)
                        for i, src in enumerate(sources):
                            mm = pe.transpose(out[:, i * P:(i + 1) * P], src, ident[:, :])
                        close_job(mm, job)

                    def product(out, pairs):
                        for i, (lhs, rhs) in enumerate(pairs):
                            mm = pe.matmul(out, lhs, rhs, start=(i == 0), stop=(i == len(pairs) - 1))
                        return mm

                    normed = [0]

                    def turn_normed(jobs2, src):
                        normed[0] += 1
                        pe.wait_ge(sems["x_normed"], normed[0])
                        for i, job in enumerate(jobs2):
                            turn(job, [src[:, (4 * i + c) * P:(4 * i + c + 1) * P] for c in range(4)])

                    def h_ready(jobs2):
                        for job in jobs2:
                            pe.wait_ge(drained[at[job] % BANKS], at[job] // BANKS + 1)

                    def rows_product(job, w, lhs):
                        close_job(product(open_job(job)[:, :], [(lhs[:, c, :], w[:, c, :]) for c in range(KC)]), job)

                    def cols_product(job, w):
                        out = open_job(job)
                        for o in range(4):
                            mm = product(out[:, o * P:(o + 1) * P],
                                         [(w[:, c, o * P:(o + 1) * P], h_t[:, c, :]) for c in range(KC)])
                        close_job(mm, job)

                    def mem_kv():
                        pe.wait_ge(sems["mem_gained"], 1)
                        for i in range(4):
                            w = need_weights(f"mk{i // 2}")
                            out = open_job(f"MK{i}")
                            for k in range(2):
                                o = (2 * i + k) % 4
                                mm = product(out[:, k * N_MEM:(k + 1) * N_MEM],
                                             [(w[:, c, o * P:(o + 1) * P], mem_g[:, c, :]) for c in range(KC)])
                            close_job(mm, f"MK{i}")
                        for i in range(4):
                            w = need_weights(f"mv{i // 2}")
                            m = i % 2
                            close_job(product(open_job(f"MV{i}")[:, :],
                                              [(mem_g[:, c, m * P:(m + 1) * P], w[:, c, :]) for c in range(KC)]),
                                      f"MV{i}")

                    def part0():
                        if first:
                            pe.wait_ge(sems["fixed_loaded"], 48)
                            for m in range(2):
                                turn_normed([f"MT{2 * m}", f"MT{2 * m + 1}"], area1[:, m * D:(m + 1) * D])
                            mem_kv()
                        turn_normed(["NT0", "NT1"], x_n)
                        h_ready(["NT0", "NT1"])
                        rows_product("ZQ", need_weights("zq"), h_t)
                        rows_product("ZK1", need_weights("zk1"), h_t)
                        rows_product("ZK2", need_weights("zk2"), h_t)
                        wg = small("wg").rearrange("p (c n) -> p c n", c=KC)
                        pe.wait_ge(sems["smalls_loaded"], 16)
                        close_job(product(open_job("GT")[:, 0:24], [(h_t[:, c, :], wg[:, c, :]) for c in range(KC)]),
                                  "GT")
                        cols_product("AB", need_weights("ab"))

                    def part1():
                        pe.wait_ge(sems["kv_rope_done"], 1)
                        turn("QT", [z[:, i * P:(i + 1) * P] for i in range(4)])
                        turn("KT", [z[:, ZC[n]:ZC[n] + P] for n in ("kc", "vc", "ks", "kw")])
                        out = open_job("PM")
                        pe.wait_ge(sems["tile_consts_loaded"], 16)
                        for g in range(4):
                            dst = out[(g % 2) * 64:(g % 2) * 64 + 64, (g // 2) * P:(g // 2 + 1) * P]
                            mm = product(dst, [
                                (z[:, ZC["pool"] + g * 64:ZC["pool"] + g * 64 + 64], tile_const("cur", g * P, P)),
                                (pool_prev[:, g * 64:g * 64 + 64], tile_const("prev", g * P, P))])
                        close_job(mm, "PM")
                        pe.wait_ge(sems["cmp_in_built"], 16)
                        out = open_job("HID")
                        for kind, name in enumerate(("ck", "cv")):
                            w = w_ring[:, slot[name] % RING, :].rearrange("p (c n) -> p c n", c=16)
                            need_weights(name)
                            for hcn in range(2):
                                o = (kind * 2 + hcn) * 32
                                mm = product(out[:, o:o + 32], [(w[:, c, hcn * P:(hcn + 1) * P], cmp_in[:, kind, c, :])
                                                                for c in range(16)])
                        close_job(mm, "HID")
                        pe.wait_ge(sems["cmp_hidden"], 1)
                        pe.wait_ge(drained[at["HID"] % BANKS], at["HID"] // BANKS + 1)
                        out = open_job("KC")
                        w2 = small("w2").rearrange("p (k c d) -> p k c d", k=2, c=2)
                        for kvh in range(KV_HEADS):
                            product(out[kvh * HD:(kvh + 1) * HD, 0:NC],
                                    [(w2[:, 0, c, :], hid_k[:, c, kvh * NC:(kvh + 1) * NC]) for c in range(2)])
                        for kvh in range(KV_HEADS):
                            mm = product(out[:, NC + kvh * HD:NC + (kvh + 1) * HD],
                                         [(hid_v[:, 2 * c + kvh, :, :].rearrange("p h n -> p (h n)"), w2[:, 1, c, :])
                                          for c in range(2)])
                        close_job(mm, "KC")

                    def head_rows(h):
                        return slice((h // 4) * HD, (h // 4 + 1) * HD)

                    def scores(prefix, kind):
                        for i in range(4):
                            out = open_job(f"{prefix}{i}")
                            for k in range(2):
                                h = (i % 2) * 4 + 2 * (i // 2) + k
                                mm = product(out[:, k * S:(k + 1) * S],
                                             [(q_t[head_rows(h), h % 4, :], kv_t[head_rows(h), kind, 0:S])])
                            close_job(mm, f"{prefix}{i}")

                    def turn_probs(prefix, done):
                        order = [(i % 2) * 4 + 2 * (i // 2) + k for i in range(4) for k in range(2)]
                        for i in range(4):
                            h = [2 * i, 2 * i + 1]
                            pe.wait_ge(sems[done], max(order.index(n) for n in h) + 1)
                            turn(f"{prefix}{i}", [probs[:, n, c * P:(c + 1) * P] for n in h for c in range(2)])

                    def weighted(job, kind, turned):
                        pe.wait_ge(sems[turned], 4)
                        out = open_job(job)
                        for h in range(HEADS):
                            cols = kind * P + (h // 4) * HD
                            mm = product(out[:, h * HD:(h + 1) * HD],
                                         [(probs_t[:, h, c, :], kv_n[:, c * 256 + cols:c * 256 + cols + HD])
                                          for c in range(2)])
                        close_job(mm, job)

                    def part2():
                        pe.wait_ge(sems["q_turned"], 1)
                        pe.wait_ge(sems["k_turned"], 1)
                        pe.wait_ge(drained[at["KC"] % BANKS], at["KC"] // BANKS + 1)
                        for i in range(2):
                            out = open_job(f"SC{i}")
                            for k in range(4):
                                h = 4 * i + k
                                mm = product(out[:, k * NC:(k + 1) * NC],
                                             [(q_t[head_rows(h), k, :], cmp_kt[head_rows(h), :])])
                            close_job(mm, f"SC{i}")
                        scores("SS", 2)
                        pe.wait_ge(sems["cmp_probs_ready"], 1)
                        turn("TCM", [p_cmp[:, :, :].rearrange("p h n -> p (h n)")])
                        pe.wait_ge(sems["cmp_turned"], 1)
                        close_job(product(open_job("OC")[:, :],
                                          [(pt_cmp[:, :], cmp_vb[:, :, :].rearrange("p h d -> p (h d)"))]), "OC")

                    def part3():
                        turn_probs("TS", "sel_exp")
                        pe.wait_ge(sems["v_kept"], 1)
                        weighted("OS", 0, "sel_turned")
                        scores("SW", 3)

                    def part4():
                        turn_probs("TW", "win_exp")
                        weighted("OW", 1, "win_turned")
                        pe.wait_ge(sems["conv_out"], 2)
                        turn("CT", [conv[:, g, :] for g in range(2)])
                        pe.wait_ge(drained[at["CT"] % BANKS], at["CT"] // BANKS + 1)
                        turn("CB", [conv_n[:, g, :] for g in range(2)])
                        pe.wait_ge(sems["pool_mean"], 1)
                        out = open_job("PY")
                        pbd = small("pbd").rearrange("p (k n) -> p k n", k=2)
                        for i in range(2):
                            mm = product(out[:, i * P:(i + 1) * P], [(pbd[:, i, :], pool_m[:, i, :])])
                        close_job(mm, "PY")
                        pe.wait_ge(sems["conv_silu"], 1)
                        out = open_job("PW")
                        pw = small("pw").rearrange("p (c n) -> p c n", c=2)
                        for o in range(2):
                            mm = product(out[:, o * P:(o + 1) * P],
                                         [(pw[:, c, o * P:(o + 1) * P], conv_n[:, c, :]) for c in range(2)])
                        close_job(mm, "PW")
                        pe.wait_ge(sems["o_mixed"], 1)
                        turn("OT", [o_sum[:, c * P:(c + 1) * P] for c in range(4)])
                        pe.wait_ge(sems["cat_ready"], 1)
                        rows_product("WO0", need_weights("wo0"), cat_t)
                        rows_product("WO1", need_weights("wo1"), cat_t)

                    def part5():
                        turn_normed(["NX0", "NX1"], x_n)
                        h_ready(["NX0", "NX1"])
                        cols_product("XQ0", need_weights("xq0"))
                        cols_product("XQ1", need_weights("xq1"))
                        pe.wait_ge(sems["xq_ready"], 2)
                        for i in range(2):
                            out = open_job(f"XS{i}")
                            for k in range(2):
                                h = 2 * i + k
                                mm = product(out[:, k * N_MEM:(k + 1) * N_MEM],
                                             [(xq_t[:, 2 * h + c, :], mem_k[:, 2 * h + c, :]) for c in range(2)])
                            close_job(mm, f"XS{i}")
                        pe.wait_ge(sems["xs_probs"], 1)
                        for i in range(2):
                            turn(f"XT{i}", [x_probs[:, h, c * P:(c + 1) * P] for h in (2 * i, 2 * i + 1)
                                            for c in range(2)])
                        pe.wait_ge(sems["xs_turned"], 2)
                        for i in range(2):
                            out = open_job(f"XO{i}")
                            for k in range(4):
                                o = 4 * i + k
                                mm = product(out[:, k * P:(k + 1) * P],
                                             [(mem_v[:, m, o * P:(o + 1) * P], xprobs_t[:, o // 2, m, :])
                                              for m in range(2)])
                            close_job(mm, f"XO{i}")
                        pe.wait_ge(sems["xo_ready"], 2)
                        rows_product("XW0", need_weights("xo0"), xo_t)
                        rows_product("XW1", need_weights("xo1"), xo_t)
                        if mem_layer is not None and not first:
                            mem_kv()

                    def part6():
                        turn_normed(["NF0", "NF1"], x_n)
                        h_ready(["NF0", "NF1"])
                        for i in range(4):
                            cols_product(f"PQ{i}", need_weights(f"pq{i}"))
                        subk = small("subk").rearrange("p (e n) -> p e n", e=2)
                        for i in range(4):
                            pe.wait_ge(sems["pq_ready"], i + 1)
                            out = open_job(f"PK{i}")
                            for k in range(4):
                                j = 4 * i + k
                                mm = product(out[:, k * P:(k + 1) * P], [(pq_t[:, j, :], subk[:, j % 2, :])])
                            close_job(mm, f"PK{i}")

                    def nothing():
                        pass

                    if experts is not None:
                        for _ in range(BPE):
                            pe.sem_inc(sems["v_free_pe"], 1)
                            pe.sem_inc(sems["diag_done"], 1)
                        for c in range(2):
                            pe.matmul(acc_pe[:, c * 512:(c + 1) * 512], zero[:, :], xs[:, 0:512], start=True,
                                      stop=False, skip_group_check=True)
                    if dense is not None:
                        parts = [part0, part1, part2, part3, part4, part5, part6, nothing, nothing, nothing, nothing]
                        b0 = 0
                        for part, n in zip(parts, TURNS):
                            part()
                            if experts is not None:
                                expert_batches(b0, n)
                            b0 += n
                    else:
                        expert_batches(0, NB)

            for sem in stage_sems:
                nc.gpsimd.sem_clear(sem)
            nc.all_engine_barrier()

        pool_m = sb("pool_m", [P, 2, P])
        stage(0, None, mem_layer=0, first=True)
        stage(1, 0, mem_layer=1)
        with nc.Fori(1, STAGES - 1) as s:
            stage(s + 1, s)
        stage(None, STAGES - 1, last=True)


def columns(w):
    return w.reshape(-1, P, w.shape[-1]).transpose(1, 0, 2)


def constants():
    t = np.arange(P)
    tile_consts = np.zeros((TILES, P, N_TC), np.float32)

    def put(tile, name, value):
        at, w = TC[name]
        tile_consts[tile, :, at:at + w] = value

    for tile in range(TILES):
        tok = tile * P + t
        put(tile, "causal", np.where(np.arange(S)[None, :] <= tok[:, None], 0.0, NEG))
        n = np.arange(NC)
        ok = (n[None, :] * CMP_STRIDE + CMP_BLOCK - 1 <= tok[:, None]) & (n[None, :] < N_CMP)
        put(tile, "cadd", np.where(ok, 0.0, NEG))
        put(tile, "cvalid", ok)
        cur, prev = np.zeros((P, 4, P)), np.zeros((P, 4, P))
        for g, w in enumerate(POOL_WINDOWS):
            start = np.maximum(tok + 1 - w, 0)
            for o in range(P):
                for i in range(start[o], tok[o] + 1):
                    which = cur if i >= tile * P else prev
                    which[i % P, g, o] = np.float32(1.0 / (tok[o] + 1 - start[o])) - (1.0 if i == tok[o] else 0.0)
        put(tile, "cur", cur.reshape(P, -1))
        put(tile, "prev", prev.reshape(P, -1))
        put(tile, "flag", float(tile > 0))
    head_mask = (t[:, None] // NC == np.arange(HEADS)[None, :]).astype(np.float32)
    freqs = np.float32(THETA) ** (-np.arange(HALF, dtype=np.float32) * np.float32(2.0) / np.float32(ROT))
    return tile_consts, head_mask, freqs.astype(np.float32)


def kernel(**inputs):
    import concourse.bacc as _bacc
    from concourse.bass_utils import run_bass_kernel_spmd as _run

    given = {n: np.asarray(v) for n, v in inputs.items()}
    tile_consts, head_mask, freqs = constants()

    blocks = np.zeros((DEPTH * len(WHERE), P, KC * BLK), np.float32)
    smalls = np.zeros((DEPTH, P, N_SMALL), np.float32)
    for l in range(DEPTH):
        def put_block(name, w):
            blocks[l * len(WHERE) + WHERE[name]] = columns(w).reshape(P, -1)

        def put(name, value):
            at, w = SMALL[name]
            smalls[l, :, at:at + w] = np.asarray(value).reshape(P, w)

        w_in = given["w_in"][l]
        put_block("zq", w_in[:, 0:512].reshape(D, KV_HEADS, 4, HD).transpose(0, 2, 1, 3).reshape(D, 512))
        put_block("zk1", w_in[:, 512:1024])
        put_block("zk2", np.concatenate([w_in[:, 1024:1280], w_in[:, 1816:2072]], 1))
        put_block("ab", w_in[:, 1304:1816])
        put_block("ck", given["cmp_w1"][l, 0])
        put_block("cv", given["cmp_w1"][l, 1])
        for name, w, n in (("wo", given["w_out"][l], 2), ("xq", given["xa_wq"][l], 2), ("xo", given["xa_wo"][l], 2),
                           ("pq", given["peer_wq"][l], 4), ("mk", given["xa_wkv"][l][:, 0:D], 2),
                           ("mv", given["xa_wkv"][l][:, D:2 * D], 2)):
            for i in range(n):
                put_block(f"{name}{i}", w[:, i * BLK:(i + 1) * BLK])
        put("w2", given["cmp_w2"][l].reshape(2, 2, P, HD).transpose(2, 0, 1, 3))
        pe = given["cmp_pe"][l].reshape(2, 16, 2, HD).transpose(3, 0, 2, 1)
        put("pe", np.concatenate([pe, pe], 0))
        put("cw", given["conv_w"][l].reshape(CONV_W, 2, P).transpose(2, 1, 0))
        for name, key in (("cb", "conv_b"), ("lng", "conv_ln_g"), ("lnb", "conv_ln_b"), ("pwb", "conv_pw_b"),
                          ("psc", "pool_scale"), ("gmix", "norm_mix_g"), ("gxa", "norm_xa_g"), ("gffn", "norm_ffn_g")):
            put(name, given[key][l].reshape(-1, P).T)
        put("pw", columns(given["conv_pw_w"][l]))
        pbd = np.zeros((2, 2, 64, 2, 64), np.float32)
        for g in range(4):
            pbd[g // 2, g % 2, :, g % 2, :] = given["pool_w"][l, g]
        put("pbd", pbd.reshape(2, P, P).transpose(1, 0, 2))
        put("wg", columns(w_in[:, 1280:1304]))
        put("subk", given["peer_subkeys"][l].transpose(2, 0, 1))
        put("first", np.full((P, 1), l * EXPERTS))
    fixed = np.concatenate([
        head_mask, np.tile(np.arange(TOPK, dtype=np.float32), (P, 1)), np.tile(freqs, (P, 1)),
        given["norm_mem_g"].reshape(DEPTH, KC, P).transpose(2, 0, 1).reshape(P, DEPTH * KC)], 1)

    arrays = {
        "x": given["x"].reshape(TILES, P, D).transpose(1, 0, 2),
        "mem": given["mem"].reshape(2, P, D).transpose(1, 0, 2),
        "positions": given["positions"].reshape(TILES, P).T,
        "blocks": blocks, "smalls": smalls, "tile_consts": tile_consts,
        "ident": np.eye(P, dtype=np.float32), "fixed": fixed,
        "ffn_gain": np.tile(given["norm_ffn_g"][:, None, :], (1, P, 1)),
        "final_gain": np.tile(given["final_g"][None, :], (P, 1)),
        "u": given["peer_u"].reshape(DEPTH * EXPERTS, D), "v": given["peer_v"].reshape(DEPTH * EXPERTS, D),
    }
    nc = _bacc.Bacc("TRN2", target_bir_lowering=False, num_devices=1)
    args, sent = {}, {}
    for name, value in arrays.items():
        value = np.ascontiguousarray(value)
        sent[f"{name}_in"] = value
        args[name] = nc.dram_tensor(f"{name}_in", value.shape, mybir.dt.from_np(value.dtype),
                                    kind="ExternalInput").ap()
    args["out"] = nc.dram_tensor("hidden_out", (S, D), F32, kind="ExternalOutput").ap()
    build_program(nc, args)
    result = _run(nc, [sent], core_ids=[0])
    return result.results[0]["hidden_out"].reshape(1, S, D)
```

```python
from contextlib import ExitStack
import math

import numpy as np

import concourse.bass as bass
from concourse import mybir

F32 = mybir.dt.float32
I32 = mybir.dt.int32
U32 = mybir.dt.uint32
ALU = mybir.AluOpType
ACT = mybir.ActivationFunctionType
AX = mybir.AxisListType

P = 128
D = 1024
KC = D // P
TILES = 2
S = TILES * P
DEPTH = 2
STAGES = DEPTH * TILES
N_MEM = 256
HEADS, KV_HEADS, HD = 8, 2, 64
CMP_BLOCK, CMP_STRIDE, CMP_HIDDEN = 32, 16, 256
N_CMP = (S - CMP_BLOCK) // CMP_STRIDE + 1
NC = 16
CONV_W = 31
HIST = CONV_W - 1
POOL_WINDOWS = (2, 4, 8, 16)
XH = 4
PH, PK, TOPK = 8, 128, 16
EXPERTS = PK * PK
PAIRS = PH * TOPK
EPS = 1e-6
NEG = -1e30
LOWEST = -3.0e38
THETA, ROT = 500000.0, HD // 4
HALF = ROT // 2

B = 8
NB = PAIRS // B
QUARTER = NB // 4
BPE = 5
BDV = B - BPE
V_ORDER = list(range(B))
BLK = 512
RING = 2

ZC = {"q": 0, "kc": 512, "vc": 640, "ks": 768, "vs": 896, "kw": 1024, "vw": 1152, "pool": 1280}
ZW = 1536

SMALL = {}
_n = 0
for _name, _w in (("w2", 256), ("pe", 64), ("cw", 2 * CONV_W), ("cb", 2), ("lng", 2), ("lnb", 2), ("pwb", 2),
                  ("psc", 2), ("pw", 512), ("pbd", 256), ("wg", 192), ("gmix", 8), ("gxa", 8), ("gffn", 8),
                  ("subk", 256), ("first", 1)):
    SMALL[_name] = (_n, _w)
    _n += _w
N_SMALL = _n

TC = {}
_n = 0
for _name, _w in (("causal", S), ("cadd", NC), ("cvalid", NC), ("cur", 4 * P), ("prev", 4 * P), ("flag", 1)):
    TC[_name] = (_n, _w)
    _n += _w
N_TC = _n

BLOCKS = ["ab", "zq", "zk1", "zk2", "ck", "cv", "wo0", "wo1", "xq0", "xq1", "xo0", "xo1", "pq0", "pq1", "pq2", "pq3"]
MEM_BLOCKS = ["mk0", "mk1", "mv0", "mv1"]
WHERE = {n: i for i, n in enumerate(BLOCKS + MEM_BLOCKS)}

STEP_JOBS = {
    "mem_norm": ["MT0", "MT1", "MT2", "MT3"], "mix_norm": ["NT0", "NT1"], "ab": ["AB"], "zq": ["ZQ"], "zk1": ["ZK1"],
    "zk2": ["ZK2"], "branch_gates": ["GT"], "turn_kv": ["KT", "QT", "PM"], "cmp_hidden": ["HID"],
    "cmp_hidden_turn": ["HT"], "cmp_kv": ["KC"],
    "sel_scores": ["SS0", "SS1", "SS2", "SS3"], "cmp_scores": ["SC0", "SC1"], "cmp_probs": ["TCM"],
    "sel_turn": ["TS0", "TS1", "TS2", "TS3"], "cmp_out": ["OC"], "sel_out": ["OS"],
    "win_scores": ["SW0", "SW1", "SW2", "SW3"], "win_turn": ["TW0", "TW1", "TW2", "TW3"], "win_out": ["OW"],
    "conv_norm": ["CT"], "conv_act": ["CB"], "small_branches": ["PY", "PW"], "mix_turn": ["OT"], "wo0": ["WO0"],
    "wo1": ["WO1"], "xa_norm": ["NX0", "NX1"], "xq0": ["XQ0"], "xq1": ["XQ1"], "xa_scores": ["XS0", "XS1"],
    "xa_turn": ["XT0", "XT1"], "xa_out": ["XO0", "XO1"], "xo0": ["XW0"], "xo1": ["XW1"],
    "mem_kv0": ["MK0"], "mem_kv1": ["MK1"], "mem_kv2": ["MK2"], "mem_kv3": ["MK3"],
    "mem_kv4": ["MV0"], "mem_kv5": ["MV1"], "mem_kv6": ["MV2"], "mem_kv7": ["MV3"],
    "ffn_norm": ["NF0", "NF1"], "pq0": ["PQ0"], "pq1": ["PQ1"], "pq2": ["PQ2"], "pq3": ["PQ3"],
    "sub_scores0": ["PK0"], "sub_scores1": ["PK1"], "sub_scores2": ["PK2"], "sub_scores3": ["PK3"],
}
JOB_BLOCKS = {"AB": ["ab"], "ZQ": ["zq"], "ZK1": ["zk1"], "ZK2": ["zk2"], "HID": ["ck", "cv"], "WO0": ["wo0"],
              "WO1": ["wo1"], "XQ0": ["xq0"], "XQ1": ["xq1"], "XW0": ["xo0"], "XW1": ["xo1"], "PQ0": ["pq0"],
              "PQ1": ["pq1"], "PQ2": ["pq2"], "PQ3": ["pq3"], "MK0": ["mk0"], "MK2": ["mk1"], "MV0": ["mv0"],
              "MV2": ["mv1"]}
LAST_USE = {b: job for job, names in JOB_BLOCKS.items() for b in names}
LAST_USE.update({"mk0": "MK1", "mk1": "MK3", "mv0": "MV1", "mv1": "MV3"})
BANKS = 4

PLAN = ["rank1", "rank_pairs1", "look_up1", "gates1", "rank2", "mix_norm", "ab", "rank_pairs2", "look_up2",
        "gates2", "zq", "conv_in", "conv0", "zk1", "zk2", "rope", "conv1", "turn_kv", "rank3", "rank_pairs3",
        "look_up3", "gates3", "branch_gates", "cmp_in", "cmp_hidden", "conv2", "cmp_hidden_turn", "sel_scores",
        "cmp_kv", "conv3", "cmp_scores", "cmp_probs", "cmp_out", "sel_turn", "win_scores", "sel_out", "conv_norm",
        "win_turn", "conv_act", "conv_silu", "win_out", "small_branches", "mix_turn", "wo0", "wo1", "xa_norm",
        "xq0", "xq1", "xa_scores", "xa_turn", "xa_out", "xo0", "xo1", "ffn_norm", "pq0", "sub_scores0", "rank0",
        "pq1", "pq2", "sub_scores1", "rank_pairs0", "look_up0", "sub_scores2", "gates0", "pq3", "sub_scores3"]
MEM_PLAN = ["rank1", "rank_pairs1", "mix_norm", "gates1", "ab", "look_up1", "rank2", "conv_in", "rank_pairs2",
            "conv0", "gates2", "look_up2", "zq", "conv1", "zk1", "zk2", "rope", "conv2", "turn_kv", "rank3",
            "rank_pairs3", "branch_gates", "gates3", "look_up3", "cmp_in", "cmp_hidden", "conv3", "cmp_hidden_turn",
            "cmp_kv", "cmp_scores", "cmp_probs", "sel_scores", "sel_turn", "conv_norm", "conv_act", "cmp_out",
            "conv_silu", "sel_out", "win_scores", "small_branches", "win_turn", "win_out", "mix_turn", "wo0", "wo1",
            "xa_norm", "xq0", "xq1", "xa_scores", "xa_turn", "xa_out", "mem_gain", "xo0", "mem_kv0", "mem_kv1",
            "mem_kv2", "mem_kv3", "mem_kv4", "mem_kv5", "xo1", "mem_kv6", "mem_kv7", "ffn_norm", "pq0",
            "sub_scores0", "pq1", "rank0", "pq2", "sub_scores1", "sub_scores2", "rank_pairs0", "gates0", "look_up0",
            "pq3", "sub_scores3"]
FIRST_PLAN = ["mix_norm", "zq", "rope_tables", "ab", "conv_in", "mem_norm", "zk1", "conv0", "conv1", "mem_gain",
              "zk2", "rope", "branch_gates", "turn_kv", "cmp_in", "conv2", "cmp_hidden", "conv3", "cmp_hidden_turn",
              "cmp_kv", "cmp_scores", "sel_scores", "mem_kv0", "mem_kv1", "sel_turn", "mem_kv2", "cmp_probs",
              "mem_kv3", "mem_kv4", "conv_norm", "mem_kv5", "conv_act", "win_scores", "cmp_out", "sel_out",
              "win_turn", "conv_silu", "win_out", "small_branches", "mix_turn", "wo0", "wo1", "xa_norm", "xq0",
              "xq1", "xa_scores", "mem_kv6", "xa_turn", "mem_kv7", "xa_out", "xo0", "xo1", "ffn_norm", "pq0",
              "sub_scores0", "rank0", "rank_pairs0", "pq1", "look_up0", "sub_scores1", "pq2", "gates0",
              "sub_scores2", "pq3", "sub_scores3"]
LAST_PLAN = ["rank1", "rank_pairs1", "gates1", "look_up1", "rank2", "rank_pairs2", "gates2", "look_up2", "rank3",
             "rank_pairs3", "gates3", "look_up3"]

def turns(vector, tensor):
    return {"vector": vector, "scalar": vector, "tensor": tensor}


TURNS = turns({"rank1": 1, "mix_norm": 1, "look_up2": 1, "cmp_hidden": 1, "cmp_kv": 2, "sel_turn": 1, "win_scores":
               1, "win_turn": 1, "xq0": 1, "xa_out": 1, "xo0": 1, "pq0": 1, "sub_scores2": 1, "sub_scores3": 1},
              {"start": 1, "zq": 1, "rank_pairs3": 1, "cmp_hidden_turn": 1, "conv3": 1, "sel_turn": 1, "win_scores":
               1, "win_out": 2, "xa_scores": 1, "xo1": 1, "rank0": 1, "sub_scores1": 1, "pq3": 1, "sub_scores3": 1})
MEM_TURNS = turns({"start": 1, "ab": 1, "conv0": 1, "rope": 1, "conv3": 1, "cmp_probs": 1, "sel_turn": 1,
                   "conv_silu": 1, "win_turn": 1, "xq0": 1, "mem_gain": 1, "mem_kv3": 1, "xo1": 1, "pq1": 1, "pq2":
                   1},
                  {"conv1": 2, "branch_gates": 1, "gates3": 1, "cmp_hidden_turn": 1, "sel_turn": 1, "cmp_out": 1,
                   "win_turn": 1, "wo1": 1, "xq1": 1, "mem_kv1": 1, "mem_kv3": 1, "sub_scores0": 1, "gates0": 1,
                   "pq3": 1})
LAST_TURNS = turns({"start": 1, "rank1": 1, "rank2": 2, "rank3": 2, "rank_pairs3": 2, "gates3": 2, "look_up3": 5},
                   {"start": 1, "rank1": 1, "look_up1": 1, "rank2": 1, "gates2": 1, "look_up2": 2, "rank3": 1,
                    "rank_pairs3": 2, "gates3": 1, "look_up3": 4})

TURN_PARTS = [6.25]
for _bits in (10, 20):
    TURN_PARTS.append(round((2 * math.pi - sum(TURN_PARTS)) * 2 ** _bits) / 2 ** _bits)
TURN_PARTS.append(2 * math.pi - sum(TURN_PARTS))
ROUNDER = 1.5 * 2 ** 23

SIGNALS = [
    "tile_consts_loaded", "smalls_loaded", "fixed_loaded", "ident_loaded", "mem_loaded", "ffn_gain_loaded",
    "x_loaded", "out_stored",
    "vector_step", "kv_rope_done", "cmp_in_built", "h_scaled", "cmp_max_taken", "cmp_probs_ready",
    "sel_scored", "win_scored", "o_mixed", "conv_out", "conv_var", "conv_affine", "conv_silu",
    "x_mixed", "x_attended", "norm_var", "norm_rstd", "xs_max", "xs_probs", "experts_ranked", "mem_gained",
    "rope_reduced", "zeroed", "routed",
    "scalar_step", "norm_squares", "norm_std", "x_normed", "z_copied", "gate_exp", "b_exp", "q_turned",
    "k_turned", "v_kept", "pool_kept", "cmp_hidden", "cmp_exp", "cmp_turned", "sel_exp", "sel_turned", "win_exp",
    "win_turned", "pool_mean", "conv_std", "conv_exp", "cat_ready", "xq_ready", "xs_exp", "xs_turned", "xo_ready",
    "pq_ready", "pk_ready", "gate_exps", "mem_turned", "mem_k_ready", "mem_v_ready", "rope_sin",
    "first_routed", "idx_staged", "gathers_issued", "h_taken", "u_free", "v_free_pe", "v_free_dv",
    "gelu_done", "weights_done", "diag_done", "sum_zeroed", "experts_added", "out_ready",
    "final_var", "final_std",
]


def build_program(nc, a):
    with ExitStack() as ctx:
        def sb(name, shape, dt=F32):
            return ctx.enter_context(nc.sbuf_tensor(name, shape, dt))

        def psum(name, shape):
            return ctx.enter_context(nc.psum_tensor(name, shape, F32))

        u_rows = sb("u_rows", [P, B, D])
        v_rows = sb("v_rows", [P, B, D])
        w_ring = sb("w_ring", [P, RING, KC * BLK])
        mem_k = sb("mem_k", [P, KC, N_MEM])
        mem_v = sb("mem_v", [P, 2, D])
        mem_t = sb("mem_t", [P, KC, N_MEM])
        xs = sb("xs", [P, TILES * D])
        h_t = sb("h_t", [P, KC, P])
        area1 = sb("area1", [P, 2048])
        area2 = sb("area2", [P, 2048])
        area3 = sb("area3", [P, 2048])
        kv_t = sb("kv_t", [P, 4, S + NC])
        kv_n = sb("kv_n", [P, TILES * 256])
        pool_prev = sb("pool_prev", [P, 256])
        q_t = sb("q_t", [P, 4, P])
        hid_k = sb("hid_k", [P, 2, 32])
        cmp_kt = sb("cmp_kt", [P, NC])
        cmp_vb = sb("cmp_vb", [P, HEADS, HD])
        p_cmp = sb("p_cmp", [P, HEADS, NC])
        pt_cmp = sb("pt_cmp", [P, P])
        h_ffn = sb("h_ffn", [P, D])
        hc = sb("hc", [P, 2, HIST + P])
        conv = sb("conv", [P, 2, P])
        conv_u = sb("conv_u", [P, 2, P])
        conv_e = sb("conv_e", [P, 2, P])
        smalls = sb("smalls", [P, N_SMALL])
        tcon = sb("tcon", [P, N_TC])
        acc_dv = sb("acc_dv", [P, D])
        diag = sb("diag", [P, 2 * BPE, P])
        ident = sb("ident", [P, P])
        zero = sb("zero", [P, P])
        fixed = sb("fixed", [P, HEADS + TOPK + HALF + 2 * KC])
        head_mask, iota16, freqs = fixed[:, 0:8], fixed[:, 8:24], fixed[:, 24:32]
        gain_mem = fixed[:, 32:48]
        pos = sb("pos", [P, TILES], I32)
        cos_t = sb("cos_t", [P, TILES * 20 * HALF])
        sin_t = sb("sin_t", [P, TILES * 20 * HALF])
        gates = sb("gates", [P, 24])
        st = sb("st", [P, 96])
        idx = sb("idx", [P, PAIRS], I32)
        idx_batch = sb("idx_batch", [P, 2 * B], I32)
        expert_base = sb("expert_base", [P, 1])
        gate = sb("gate", [P, PAIRS])
        act_b = sb("act_b", [P, B])
        gelu_b = sb("gelu_b", [P, B])
        wgt_b = sb("wgt_b", [P, B])
        half_i = sb("half_i", [P, 16, TOPK], U32)
        half_v = sb("half_v", [P, 16, TOPK])
        top_v = sb("top_v", [P, PH, TOPK])
        top_p = sb("top_p", [P, PH, TOPK], U32)

        h_ps = psum("h_ps", [P, D])
        acc_pe = psum("acc_pe", [P, D])
        bank = [psum(f"bank{i}", [P, BLK]) for i in range(BANKS)]

        x_n = area2[:, 0:D]
        probs = area1[:, :].rearrange("p (h k) -> p h k", h=HEADS)
        x_probs = area1[:, 0:XH * N_MEM].rearrange("p (h k) -> p h k", h=XH)
        half_s = area1[:, :].rearrange("p (j n) -> p j n", j=16)
        cmp_in = area2[:, 0:1024].rearrange("p (k c n) -> p k c n", k=2, c=16)
        probs_t = area2[:, :].rearrange("p (h c t) -> p h c t", h=HEADS, c=2)
        xprobs_t = area2[:, 0:1024].rearrange("p (h c t) -> p h c t", h=XH, c=2)
        mem_g_area = area2[:, :].rearrange("p (c m) -> p c m", c=KC)
        pq_t = area2[:, :].rearrange("p (j t) -> p j t", j=16)
        z = area3[:, 0:ZW]
        xq_t = area3[:, 0:D].rearrange("p (c t) -> p c t", c=KC)
        hid_rows = area2[:, 1536:2048]
        hid_v = area2[:, 1024:1536].rearrange("p (c h n) -> p c h n", c=4, h=HEADS)
        o_sum, o_one = area3[:, 1024:1536], area3[:, 1536:2048]
        junk = h_t[:, :, :].rearrange("p c t -> p (c t)")
        cat_t = h_t
        rope_tmp = [area2[:, 1024 + 160 * i:1184 + 160 * i].rearrange("p (h d) -> p h d", h=20) for i in range(4)]
        xo_t = cat_t

        u_landed = [ctx.enter_context(nc.semaphore(f"u_landed{j}")) for j in range(B)]
        v_landed = [ctx.enter_context(nc.semaphore(f"v_landed{j}")) for j in range(B)]
        sems = {n: ctx.enter_context(nc.semaphore(n)) for n in SIGNALS}
        w_landed = [ctx.enter_context(nc.semaphore(f"w_landed{j}")) for j in range(RING)]
        filled = [ctx.enter_context(nc.semaphore(f"bank_filled{j}")) for j in range(BANKS)]
        drained = [ctx.enter_context(nc.semaphore(f"bank_drained{j}")) for j in range(BANKS)]
        stage_sems = sorted(sem.num for sem in (*sems.values(), *w_landed, *filled, *drained))
        assert stage_sems[-1] - stage_sems[0] == len(stage_sems) - 1

        def small(name, lo=0, n=None):
            at, w = SMALL[name]
            return smalls[:, at + lo:at + (w if n is None else lo + n)]

        def tile_const(name, lo=0, n=None):
            at, w = TC[name]
            return tcon[:, at + lo:at + (w if n is None else lo + n)]

        def stage(dense, experts, mem_layer=None, first=False, last=False):
            plan = LAST_PLAN if last else FIRST_PLAN if first else PLAN if mem_layer is None else MEM_PLAN
            turns = {} if first else LAST_TURNS if last else TURNS if mem_layer is None else MEM_TURNS
            jobs = [job for name in plan for job in STEP_JOBS.get(name, ())]
            blocks = [b for job in jobs for b in JOB_BLOCKS.get(job, ())]
            if dense is not None:
                layer, tile = dense // TILES, dense % TILES
            at = {n: i for i, n in enumerate(jobs)}
            slot = {n: i for i, n in enumerate(blocks)}
            last_use = {b: LAST_USE[b] for b in blocks}
            etile = experts % TILES if experts is not None else None
            mem_g = v_rows[:, 0:2, :].rearrange("p a (c m) -> p (a c) m", m=N_MEM) if first else mem_g_area
            mem_raw = u_rows[:, 0:2, :]

            def ranked(q):
                return q if q else 1 if first else 4

            def landed(b):
                return (experts * NB + b) * 16 + 16

            def bank_of(job):
                return bank[at[job] % BANKS]

            def wait_filled(eng, job):
                eng.wait_ge(filled[at[job] % BANKS], at[job] // BANKS + 1)

            def wait_drained(eng, job):
                eng.wait_ge(drained[at[job] % BANKS], at[job] // BANKS + 1)

            def drain(ins, job):
                ins.then_inc(drained[at[job] % BANKS], 1)

            def weights(name):
                return w_ring[:, slot[name] % RING, :].rearrange("p (c n) -> p c n", c=KC)

            class Steps:

                def __init__(self, eng, sem):
                    self.eng, self.sem, self.n = eng, sem, 0

                def mark(self, ins):
                    ins.then_inc(self.sem, 1)
                    self.n += 1

                def settle(self, back=0):
                    if self.n - back > 0:
                        self.eng.wait_ge(self.sem, self.n - back)

                def __call__(self, ins):
                    self.mark(ins)
                    self.settle()

            def batches(eng, batch, b0, b1):
                b = b0
                while b < b1:
                    pairs = (b1 - b) // 2
                    if b > 0 and b % 2 == 0 and pairs > 1:
                        with eng.Fori(b // 2, b // 2 + pairs) as b2:
                            for k in range(2):
                                batch(b2 * 2 + k, k)
                        b += 2 * pairs
                    else:
                        batch(b, b % 2)
                        b += 1

            def run(eng, name, steps, batch):
                b = 0
                for step_name in ["start"] + plan:
                    if step_name in steps:
                        steps[step_name]()
                    n = turns.get(name, {}).get(step_name, 0)
                    if n:
                        batches(eng, batch, b, b + n)
                        b += n
                if experts is not None:
                    batches(eng, batch, b, NB)

            with nc.Block(no_gpsimd_drain=not last) as block:

                @block.sync
                def _(sp):
                    def load_x():
                        sp.dma_start(xs[:, :].rearrange("p (t d) -> p t d", t=TILES), a["x"]).then_inc(
                            sems["x_loaded"], 16)

                    if first:
                        load_x()
                        sp.dma_start(ident[:, :], a["ident"]).then_inc(sems["ident_loaded"], 16)
                    if dense is not None:
                        sp.dma_start(smalls[:, :], a["smalls"][bass.ds(layer, 1), :, :].rearrange(
                            "a p n -> (a p) n")).then_inc(sems["smalls_loaded"], 16)
                        sp.dma_start(tcon[:, :], a["tile_consts"][bass.ds(tile, 1), :, :].rearrange(
                            "a p n -> (a p) n")).then_inc(sems["tile_consts_loaded"], 16)

                    def load_gain(source):
                        if experts is not None:
                            sp.wait_ge(sems["h_taken"], 1)
                        sp.dma_start(h_ffn[:, :], source).then_inc(sems["ffn_gain_loaded"], 16)

                    for i, name in enumerate(blocks):
                        if i >= RING:
                            wait_filled(sp, last_use[blocks[i - RING]])
                        src_layer = mem_layer if name in MEM_BLOCKS else layer
                        sp.dma_start(w_ring[:, i % RING, :],
                                     a["blocks"][bass.ds(src_layer * len(WHERE) + WHERE[name], 1), :, :].rearrange(
                                         "a p n -> (a p) n")).then_inc(w_landed[i % RING], 16)
                        if i == 1:
                            if first:
                                sp.dma_start(fixed[:, :], a["fixed"]).then_inc(sems["fixed_loaded"], 16)
                                sp.dma_start(pos[:, :], a["positions"]).then_inc(sems["fixed_loaded"], 16)
                                sp.dma_start(mem_raw, a["mem"]).then_inc(sems["mem_loaded"], 16)
                            load_gain(a["ffn_gain"][bass.ds(layer, 1), :, :].rearrange("a p n -> (a p) n"))
                    if last:
                        load_gain(a["final_gain"])
                        for t in range(TILES):
                            sp.wait_ge(sems["out_ready"], t + 1)
                            sp.dma_start(a["out"][t * P:(t + 1) * P, :], xs[:, t * D:(t + 1) * D]).then_inc(
                                sems["out_stored"], 16)
                        sp.wait_ge(sems["out_stored"], 16 * TILES)

                @block.gpsimd
                def _(pool):
                    def stage_idx(source, half):
                        nc.gpsimd.tensor_copy(idx_batch[:, half * B:(half + 1) * B], source).then_inc(
                            sems["idx_staged"], 1)

                    def gather(b, half, staged):
                        pool.wait_ge(sems["idx_staged"], staged)
                        pool.sem_inc(sems["gathers_issued"], 1)
                        for j in range(B):
                            if b is not None:
                                pool.wait_ge(sems["u_free"], b * B - B + j + 1)
                                pool.sem_inc(sems["gathers_issued"], 1)
                            row = idx_batch[:, half * B + j:half * B + j + 1].bitcast(U32)
                            nc.gpsimd.indirect_dma_start(
                                u_rows[:, j, :], None, a["u"],
                                bass.IndirectOffsetOnAxis(ap=row, axis=0)).then_inc(u_landed[j], 16)
                        for j in V_ORDER:
                            if b is not None:
                                if j < BPE:
                                    pool.wait_ge(sems["v_free_pe"], (b + 1) * BPE + j + 1)
                                else:
                                    pool.wait_ge(sems["v_free_dv"], (b - 1) * BDV + j - BPE + 1)
                                pool.sem_inc(sems["gathers_issued"], 1)
                            row = idx_batch[:, half * B + j:half * B + j + 1].bitcast(U32)
                            nc.gpsimd.indirect_dma_start(
                                v_rows[:, j, :], None, a["v"],
                                bass.IndirectOffsetOnAxis(ap=row, axis=0)).then_inc(v_landed[j], 16)

                    def next_batch(b, k):
                        stage_idx(idx[:, bass.ds(b * B, B)], k % 2)
                        gather(b, k % 2, b)

                    if experts is not None:
                        for b in range(1, QUARTER):
                            next_batch(b, b)
                        with pool.Fori(1, 4) as q:
                            pool.wait_ge(sems["routed"], q)
                            for k in range(QUARTER):
                                next_batch(q * QUARTER + k, k)
                    if not last:
                        pool.wait_ge(sems["first_routed"], 1)
                        stage_idx(idx[:, 0:B], 0)
                        if experts is not None:
                            gather(NB, 0, NB)
                        else:
                            gather(None, 0, 1)

                @block.vector
                def _(dve):
                    v = nc.vector
                    step = Steps(dve, sems["vector_step"])

                    def v_sums(b):
                        for j in range(BPE, B):
                            dve.wait_ge(v_landed[j], landed(b))
                            v.scalar_tensor_tensor(out=acc_dv[:, :], in0=v_rows[:, j, :],
                                                   scalar=wgt_b[:, j:j + 1], in1=acc_dv[:, :],
                                                   op0=ALU.mult, op1=ALU.add).then_inc(sems["v_free_dv"], 1)
                            dve.wait_ge(sems["v_free_dv"], b * BDV + j - BPE + 1)

                    def expert_batch(b, half):
                        if not (isinstance(b, int) and b == 0):
                            v_sums(b - 1)
                        for j in range(B):
                            dve.wait_ge(u_landed[j], landed(b))
                            v.tensor_tensor_reduce(u_rows[:, j, :], u_rows[:, j, :], h_ps[:, :], 1.0, 0.0,
                                                   ALU.mult, ALU.add, act_b[:, j:j + 1]).then_inc(sems["u_free"], 1)
                        dve.wait_ge(sems["gelu_done"], b + 1)
                        v.tensor_tensor(wgt_b[:, :], gelu_b[:, :], gate[:, bass.ds(b * B, B)],
                                        ALU.mult).then_inc(sems["weights_done"], 1)
                        dve.wait_ge(sems["weights_done"], b + 1)

                    def experts_start():
                        v.tensor_copy(h_ps[:, :], h_ffn[:, :]).then_inc(sems["h_taken"], 1)
                        v.memset(acc_dv[:, :], 0.0).then_inc(sems["sum_zeroed"], 1)
                        dve.wait_ge(sems["h_taken"], 1)
                        dve.wait_ge(sems["sum_zeroed"], 1)

                    def experts_end():
                        v_sums(NB - 1)
                        rows = xs[:, bass.ds(etile * D, D)]
                        step(v.tensor_tensor(rows, rows, acc_dv[:, :], ALU.add))
                        dve.wait_ge(sems["v_free_pe"], BPE * (NB + 2))
                        v.tensor_tensor(rows, rows, acc_pe[:, :], ALU.add).then_inc(sems["experts_added"], 1)
                        dve.wait_ge(sems["experts_added"], 1)

                    norms = [0]

                    def norm_tail():
                        norms[0] += 1
                        dve.wait_ge(sems["norm_squares"], norms[0])
                        v.tensor_scalar(st[:, 1:2], st[:, 0:1], 1.0 / D, EPS, ALU.mult, ALU.add).then_inc(
                            sems["norm_var"], 1)
                        dve.wait_ge(sems["norm_std"], norms[0])
                        v.reciprocal(st[:, 3:4], st[:, 2:3]).then_inc(sems["norm_rstd"], 1)

                    def gain_rows(jobs2, gain):
                        for i, job in enumerate(jobs2):
                            wait_filled(dve, job)
                            ins = v.tensor_tensor(
                                h_t[:, 4 * i:4 * i + 4, :], bank_of(job)[:, :].rearrange("p (c t) -> p c t", c=4),
                                small(gain, 4 * i, 4).unsqueeze(2).to_broadcast([P, 4, P]), ALU.mult)
                            drain(ins, job)

                    def rope_tables():
                        pf = st[:, 64:66]
                        ang, tmp, turns = st[:, 8:24], st[:, 24:40], st[:, 40:56]
                        dve.wait_ge(sems["fixed_loaded"], 32)
                        step(v.tensor_copy(pf, pos[:, :]))
                        for t in range(TILES):
                            step(v.tensor_scalar(ang[:, 8 * t:8 * t + 8], freqs, pf[:, t:t + 1], None, ALU.mult))
                        for scale in (4096.0, 1.0):
                            step(v.tensor_scalar(turns, ang, 1.0 / (2 * math.pi * scale), None, ALU.mult))
                            step(v.tensor_scalar(turns, turns, ROUNDER, ROUNDER, ALU.add, ALU.subtract))
                            for part in TURN_PARTS:
                                step(v.scalar_tensor_tensor(out=ang, in0=turns, scalar=-part * scale, in1=ang,
                                                            op0=ALU.mult, op1=ALU.add))
                        step(v.tensor_scalar(tmp, ang, math.pi / 2, -2 * math.pi, ALU.is_gt, ALU.mult))
                        step(v.scalar_tensor_tensor(out=tmp, in0=ang, scalar=math.pi / 2, in1=tmp,
                                                    op0=ALU.add, op1=ALU.add))
                        lim = 3.1415925
                        step(v.tensor_scalar(tmp, tmp, lim, -lim, ALU.min, ALU.max))
                        step(v.tensor_scalar(ang, ang, lim, -lim, ALU.min, ALU.max))
                        step(v.memset(cos_t[:, :], 1.0))
                        v.memset(sin_t[:, :], 0.0).then_inc(sems["rope_reduced"], 1)
                        dve.wait_ge(sems["rope_sin"], 2)
                        for t in range(TILES):
                            for table, src in ((cos_t, tmp), (sin_t, ang)):
                                heads = table[:, t * 160:(t + 1) * 160].rearrange("p (h d) -> p h d", h=20)
                                for lo, n in ((0, 10), (12, 2), (16, 2)):
                                    step.mark(v.tensor_copy(
                                        heads[:, lo:lo + n, :],
                                        src[:, 8 * t:8 * t + 8].unsqueeze(1).to_broadcast([P, n, HALF])))
                        step.settle()

                    def start():
                        if experts is not None:
                            experts_start()
                        if first:
                            for area in (kv_t[:, :, :], kv_n[:, :], hc[:, :, :], pool_prev[:, :]):
                                step.mark(v.memset(area, 0.0))
                            v.memset(zero[:, :], 0.0).then_inc(sems["zeroed"], 1)

                    def mem_norm():
                        norm_tail()
                        norm_tail()
                        dve.wait_ge(sems["fixed_loaded"], 32)

                    def mem_gain():
                        if first:
                            dve.wait_ge(sems["mem_turned"], 4)
                        else:
                            wait_filled(dve, "XO1")
                        v.tensor_tensor(mem_g, mem_t[:, :, :],
                                        gain_mem[:, mem_layer * KC:(mem_layer + 1) * KC].unsqueeze(2).to_broadcast(
                                            [P, KC, N_MEM]), ALU.mult).then_inc(sems["mem_gained"], 1)

                    def mix_norm():
                        norm_tail()
                        dve.wait_ge(sems["smalls_loaded"], 16)
                        dve.wait_ge(sems["tile_consts_loaded"], 16)
                        gain_rows(["NT0", "NT1"], "gmix")

                    def conv_in():
                        step(v.tensor_scalar(hc[:, :, 0:HIST], hc[:, :, P:P + HIST], tile_const("flag"), None,
                                             ALU.mult))
                        dve.wait_ge(sems["b_exp"], 1)
                        step(v.tensor_scalar(conv_e[:, :, :], conv_e[:, :, :], 1.0, None, ALU.add))
                        step(v.reciprocal(conv_e[:, :, :], conv_e[:, :, :]))
                        ins = v.tensor_tensor(hc[:, :, HIST:HIST + P],
                                              bank_of("AB")[:, 0:256].rearrange("p (g t) -> p g t", g=2),
                                              conv_e[:, :, :], ALU.mult)
                        drain(ins, "AB")
                        wait_drained(dve, "AB")

                    def conv_taps(lo, hi):
                        for k in range(lo, hi):
                            for g in range(2):
                                step.settle(1)
                                if k == 0:
                                    ins = v.tensor_scalar(conv[:, g, :], hc[:, g, 0:P], small("cw", g * CONV_W, 1),
                                                          small("cb", g, 1), ALU.mult, ALU.add)
                                else:
                                    ins = v.scalar_tensor_tensor(out=conv[:, g, :], in0=hc[:, g, k:k + P],
                                                                 scalar=small("cw", g * CONV_W + k, 1),
                                                                 in1=conv[:, g, :], op0=ALU.mult, op1=ALU.add)
                                step.mark(ins)
                        step.settle()
                        if hi == CONV_W:
                            dve.sem_inc(sems["conv_out"], 1)

                    def rope():
                        dve.wait_ge(sems["z_copied"], 3)
                        turn = [z[:, 0:1280].rearrange("p (h d) -> p h d", h=20)[:, :, i * HALF:(i + 1) * HALF]
                                for i in range(2)]
                        c = cos_t[:, bass.ds(tile * 160, 160)].rearrange("p (h d) -> p h d", h=20)
                        s = sin_t[:, bass.ds(tile * 160, 160)].rearrange("p (h d) -> p h d", h=20)
                        for tmp, (i, table) in zip(rope_tmp, ((0, c), (1, s), (0, s), (1, c))):
                            step.mark(v.tensor_tensor(tmp, turn[i], table, ALU.mult))
                        step.settle()
                        step.mark(v.tensor_tensor(turn[0], rope_tmp[0], rope_tmp[1], ALU.subtract))
                        v.tensor_tensor(turn[1], rope_tmp[2], rope_tmp[3], ALU.add).then_inc(sems["kv_rope_done"], 1)
                        step.settle()

                    def branch_gates():
                        dve.wait_ge(sems["gate_exp"], 1)
                        step(v.tensor_scalar(gates[:, :], gates[:, :], 1.0, None, ALU.add))
                        step(v.reciprocal(gates[:, :], gates[:, :]))

                    def cmp_inputs():
                        dve.wait_ge(sems["k_turned"], 1)
                        at_pe, _ = SMALL["pe"]
                        for kind in range(2):
                            for kvh in range(KV_HEADS):
                                rows = slice(kvh * HD, (kvh + 1) * HD)
                                for half in range(2):
                                    out = cmp_in[half * HD:(half + 1) * HD, kind, :, kvh * NC:(kvh + 1) * NC]
                                    for hi in range(2):
                                        tok = kv_t[rows, kind, hi * CMP_STRIDE:hi * CMP_STRIDE + S].rearrange(
                                            "p (n c e) -> p c n e", c=8, e=2)[:, :, :, half]
                                        pe_at = at_pe + kind * 32 + half * 16 + hi * 8
                                        v.tensor_tensor(
                                            out[:, hi * 8:hi * 8 + 8, :], tok,
                                            smalls[rows, pe_at:pe_at + 8].unsqueeze(2).to_broadcast([HD, 8, NC]),
                                            ALU.add).then_inc(sems["cmp_in_built"], 1)

                    def cmp_kv():
                        wait_filled(dve, "KC")
                        step.mark(v.tensor_copy(cmp_kt[:, :], bank_of("KC")[:, 0:NC]))
                        ins = v.tensor_tensor(
                            cmp_vb[:, :, :].rearrange("p (k g) d -> p k g d", k=KV_HEADS),
                            bank_of("KC")[:, NC:NC + P].rearrange("p (k d) -> p k d", k=KV_HEADS).unsqueeze(2)
                            .to_broadcast([P, KV_HEADS, 4, HD]),
                            head_mask.rearrange("p (k g) -> p k g", k=KV_HEADS).unsqueeze(3).to_broadcast(
                                [P, KV_HEADS, 4, HD]), ALU.mult)
                        drain(ins, "KC")

                    def score_pairs(prefix, signal):
                        for i in range(4):
                            job = f"{prefix}{i}"
                            h0 = (i % 2) * 4 + 2 * (i // 2)
                            wait_filled(dve, job)
                            ins = v.scalar_tensor_tensor(
                                out=probs[:, h0:h0 + 2, :], in0=bank_of(job)[:, :].rearrange("p (h k) -> p h k", h=2),
                                scalar=HD ** -0.5, in1=tile_const("causal").unsqueeze(1).to_broadcast([P, 2, S]),
                                op0=ALU.mult, op1=ALU.add)
                            drain(ins, job)
                            wait_drained(dve, job)
                            v.tensor_reduce(st[:, 8 + h0:8 + h0 + 2], probs[:, h0:h0 + 2, :], AX.X, ALU.max,
                                            negate=True).then_inc(sems[signal], 1)

                    def gated(branch, sums):
                        co = st[:, 32:40]
                        step(v.reciprocal(co, sums))
                        step(v.tensor_tensor(co, co, gates[:, :].rearrange("p (h b) -> p h b", b=3)[:, :, branch],
                                             ALU.mult))
                        return co.unsqueeze(2).to_broadcast([P, HEADS, HD])

                    def heads_of(t):
                        return t.rearrange("p (h d) -> p h d", h=HEADS)

                    def cmp_scores():
                        for i in range(2):
                            job = f"SC{i}"
                            wait_filled(dve, job)
                            ins = v.scalar_tensor_tensor(
                                out=p_cmp[:, 4 * i:4 * i + 4, :],
                                in0=bank_of(job)[:, 0:4 * NC].rearrange("p (h n) -> p h n", h=4),
                                scalar=HD ** -0.5, in1=tile_const("cadd").unsqueeze(1).to_broadcast([P, 4, NC]),
                                op0=ALU.mult, op1=ALU.add)
                            drain(ins, job)
                            wait_drained(dve, job)
                        step(v.tensor_reduce(st[:, 16:24], p_cmp[:, :, :], AX.X, ALU.max, negate=True))
                        v.tensor_tensor(p_cmp[:, :, :], p_cmp[:, :, :],
                                        st[:, 16:24].unsqueeze(2).to_broadcast([P, HEADS, NC]), ALU.add).then_inc(
                                            sems["cmp_max_taken"], 1)

                    def cmp_probs():
                        dve.wait_ge(sems["cmp_exp"], 1)
                        step(v.tensor_reduce(st[:, 24:32], p_cmp[:, :, :], AX.X, ALU.add))
                        v.tensor_tensor(p_cmp[:, :, :], p_cmp[:, :, :],
                                        tile_const("cvalid").unsqueeze(1).to_broadcast([P, HEADS, NC]),
                                        ALU.mult).then_inc(sems["cmp_probs_ready"], 1)

                    def branch_out(job, branch, sums, out):
                        co = gated(branch, sums)
                        wait_filled(dve, job)
                        ins = v.tensor_tensor(heads_of(out), heads_of(bank_of(job)[:, :]), co, ALU.mult)
                        drain(ins, job)
                        wait_drained(dve, job)

                    def sel_out():
                        dve.wait_ge(sems["sel_exp"], HEADS)
                        branch_out("OS", 1, st[:, 40:48], o_one)
                        step(v.tensor_tensor(o_sum, o_sum, o_one, ALU.add))

                    def win_scores():
                        wait_filled(dve, "TS3")
                        score_pairs("SW", "win_scored")

                    def win_out():
                        dve.wait_ge(sems["win_exp"], HEADS)
                        branch_out("OW", 2, st[:, 48:56], o_one)
                        v.tensor_tensor(o_sum, o_sum, o_one, ALU.add).then_inc(sems["o_mixed"], 1)

                    def conv_norm():
                        wait_filled(dve, "CT")
                        ct = bank_of("CT")[:, 0:256]
                        step(v.bn_stats(st[:, 64:70], ct))
                        step(v.bn_aggr(st[:, 70:72], st[:, 64:70]))
                        v.tensor_scalar(st[:, 72:73], st[:, 71:72], EPS, None, ALU.add).then_inc(sems["conv_var"], 1)
                        dve.wait_ge(sems["conv_std"], 1)
                        step(v.reciprocal(st[:, 74:75], st[:, 73:74]))
                        ins = v.tensor_scalar(conv_u[:, :, :].rearrange("p g t -> p (g t)"), ct, st[:, 70:71],
                                              st[:, 74:75], ALU.subtract, ALU.mult)
                        drain(ins, "CT")

                    def conv_act():
                        wait_filled(dve, "CB")
                        for g in range(2):
                            ins = v.tensor_scalar(conv[:, g, :], bank_of("CB")[:, g * P:(g + 1) * P],
                                                  small("lng", g, 1), small("lnb", g, 1), ALU.mult, ALU.add)
                            if g == 0:
                                step.mark(ins)
                            else:
                                drain(ins, "CB")
                        step.settle()
                        wait_drained(dve, "CB")
                        dve.sem_inc(sems["conv_affine"], 1)

                    def conv_silu():
                        dve.wait_ge(sems["conv_exp"], 1)
                        step(v.tensor_scalar(conv_e[:, :, :], conv_e[:, :, :], 1.0, None, ALU.add))
                        step(v.reciprocal(conv_e[:, :, :], conv_e[:, :, :]))
                        v.tensor_tensor(conv_u[:, :, :], conv[:, :, :], conv_e[:, :, :], ALU.mult).then_inc(
                            sems["conv_silu"], 1)

                    def add_to_x(job, i, signal):
                        cols = xs[:, bass.ds(tile * D + i * BLK, BLK)]
                        wait_filled(dve, job)
                        drain(v.tensor_tensor(cols, cols, bank_of(job)[:, :], ALU.add), job)
                        wait_drained(dve, job)
                        dve.sem_inc(sems[signal], 1)

                    def xa_norm():
                        norm_tail()
                        gain_rows(["NX0", "NX1"], "gxa")

                    def xa_scores():
                        for i in range(2):
                            job = f"XS{i}"
                            wait_filled(dve, job)
                            step(v.tensor_reduce(st[:, 8 + 2 * i:10 + 2 * i],
                                                 bank_of(job)[:, :].rearrange("p (h k) -> p h k", h=2), AX.X, ALU.max,
                                                 negate=True))
                            v.tensor_scalar(st[:, 16 + 2 * i:18 + 2 * i], st[:, 8 + 2 * i:10 + 2 * i],
                                            (D // XH) ** -0.5, None, ALU.mult).then_inc(sems["xs_max"], 1)

                    def xa_probs():
                        dve.wait_ge(sems["xs_exp"], XH)
                        step(v.reciprocal(st[:, 24:28], st[:, 20:24]))
                        v.tensor_tensor(x_probs, x_probs, st[:, 24:28].unsqueeze(2).to_broadcast([P, XH, N_MEM]),
                                        ALU.mult).then_inc(sems["xs_probs"], 1)

                    def ffn_norm():
                        norm_tail()
                        dve.wait_ge(sems["ffn_gain_loaded"], 16)
                        dve.wait_ge(sems["x_normed"], norms[0])
                        gain_rows(["NF0", "NF1"], "gffn")
                        v.tensor_tensor(h_ffn[:, :], x_n, h_ffn[:, :], ALU.mult).then_inc(sems["h_scaled"], 1)

                    def top16(values, top, where, groups):
                        for g in groups:
                            step.mark(v.max(top[:, g, 0:8], values(g)))
                        step.settle()
                        for g in groups:
                            step.mark(v.max_index(where[:, g, 0:8], top[:, g, 0:8], values(g)))
                        step.settle()
                        for g in groups:
                            step.mark(v.match_replace(values(g), top[:, g, 0:8], values(g), LOWEST))
                        step.settle()
                        for g in groups:
                            step.mark(v.max(top[:, g, 8:16], values(g)))
                        step.settle()
                        for g in groups:
                            step.mark(v.max_index(where[:, g, 8:16], top[:, g, 8:16], values(g)))
                        step.settle()

                    def quarter_of(q):
                        sums = area3[:, q * BLK:(q + 1) * BLK].rearrange("p (h i j) -> p h i j", h=2, i=TOPK)
                        at_q = q * BLK
                        half_f = area1[:, at_q:at_q + 64].rearrange("p (h e k) -> p h e k", h=2, e=2)
                        pos_f, e_hi, top_q = (area1[:, at_q + 64 + 32 * i:at_q + 96 + 32 * i].rearrange(
                            "p (h k) -> p h k", h=2) for i in range(3))
                        return sums, half_f, pos_f, e_hi, top_q.bitcast(U32)

                    def rank_half(q):
                        if q == 0:
                            dve.wait_ge(sems["pk_ready"], 1)
                        top16(lambda g: half_s[:, g, :], half_v, half_i, range(4 * q, 4 * q + 4))

                    def rank_pairs(q):
                        cand, half_f, _, _, _ = quarter_of(q)
                        pairs = half_v[:, 4 * q:4 * q + 4, :].rearrange("p (h e) k -> p h e k", e=2)
                        shape = [P, 2, TOPK, TOPK]
                        step.mark(v.tensor_tensor(cand, pairs[:, :, 0, :].unsqueeze(3).to_broadcast(shape),
                                                  pairs[:, :, 1, :].unsqueeze(2).to_broadcast(shape), ALU.add))
                        step(v.tensor_copy(
                            half_f, half_i[:, 4 * q:4 * q + 4, :].rearrange("p (h e) k -> p h e k", e=2)))
                        top16(lambda g: cand[:, g - 2 * q, :, :].rearrange("p i j -> p (i j)"), top_v, top_p,
                              range(2 * q, 2 * q + 2))
                        heads = slice(2 * q, 2 * q + 2)
                        v.tensor_tensor(gate[:, 32 * q:32 * q + 32].rearrange("p (h k) -> p h k", h=2),
                                        top_v[:, heads, :], top_v[:, heads, 0:1].to_broadcast([P, 2, TOPK]),
                                        ALU.subtract).then_inc(sems["experts_ranked"], 1)

                    def look_up(q):
                        one_hot, half_f, pos_f, e_hi, top_q = quarter_of(q)
                        shape = [P, 2, TOPK, TOPK]
                        for e, (op, by) in enumerate(((ALU.logical_shift_right, 4), (ALU.bitwise_and, 15))):
                            step(v.tensor_scalar(top_q, top_p[:, 2 * q:2 * q + 2, :], by, None, op))
                            step(v.tensor_copy(pos_f, top_q))
                            step(v.tensor_tensor(one_hot, pos_f.unsqueeze(3).to_broadcast(shape),
                                                 iota16.unsqueeze(1).unsqueeze(1).to_broadcast(shape), ALU.is_equal))
                            step(v.tensor_tensor(one_hot, one_hot, half_f[:, :, e, :].unsqueeze(2).to_broadcast(shape),
                                                 ALU.mult))
                            step(v.tensor_reduce((e_hi, pos_f)[e], one_hot, AX.X, ALU.add))
                        if q == 0:
                            step(v.tensor_copy(expert_base[:, :], small("first")))
                        step(v.tensor_scalar(e_hi, e_hi, float(PK), expert_base[:, :], ALU.mult, ALU.add))
                        if experts is not None and q == 0:
                            dve.wait_ge(sems["idx_staged"], QUARTER - 1)
                        v.tensor_tensor(idx[:, 32 * q:32 * q + 32].rearrange("p (h k) -> p h k", h=2), e_hi,
                                        pos_f, ALU.add).then_inc(sems["routed" if q else "first_routed"], 1)

                    def expert_gates(q):
                        dve.wait_ge(sems["gate_exps"], ranked(q))
                        g3 = gate[:, 32 * q:32 * q + 32].rearrange("p (h k) -> p h k", h=2)
                        step(v.tensor_reduce(st[:, 76:78], g3, AX.X, ALU.add))
                        step(v.reciprocal(st[:, 78:80], st[:, 76:78]))
                        step(v.tensor_tensor(g3, g3, st[:, 78:80].unsqueeze(2).to_broadcast([P, 2, TOPK]), ALU.mult))

                    taps = [CONV_W * i // 4 for i in range(5)]
                    steps = {
                        "start": start, "rope_tables": rope_tables, "mem_norm": mem_norm, "mem_gain": mem_gain,
                        "mix_norm": mix_norm, "conv_in": conv_in, "conv0": lambda: conv_taps(taps[0], taps[1]),
                        "conv1": lambda: conv_taps(taps[1], taps[2]), "conv2": lambda: conv_taps(taps[2], taps[3]),
                        "conv3": lambda: conv_taps(taps[3], taps[4]), "rope": rope, "branch_gates": branch_gates,
                        "cmp_in": cmp_inputs, "cmp_kv": cmp_kv,
                        "sel_scores": lambda: score_pairs("SS", "sel_scored"), "cmp_scores": cmp_scores,
                        "cmp_probs": cmp_probs, "cmp_out": lambda: branch_out("OC", 0, st[:, 24:32], o_sum),
                        "sel_out": sel_out, "win_scores": win_scores, "win_out": win_out,
                        "conv_norm": conv_norm, "conv_act": conv_act, "conv_silu": conv_silu,
                        "wo0": lambda: add_to_x("WO0", 0, "x_mixed"), "wo1": lambda: add_to_x("WO1", 1, "x_mixed"),
                        "xa_norm": xa_norm, "xa_scores": xa_scores, "xa_turn": xa_probs,
                        "xo0": lambda: add_to_x("XW0", 0, "x_attended"),
                        "xo1": lambda: add_to_x("XW1", 1, "x_attended"),
                        "ffn_norm": ffn_norm,
                    }
                    for i in range(4):
                        steps[f"rank{i}"] = lambda i=i: rank_half(i)
                        steps[f"rank_pairs{i}"] = lambda i=i: rank_pairs(i)
                        steps[f"look_up{i}"] = lambda i=i: look_up(i)
                        steps[f"gates{i}"] = lambda i=i: expert_gates(i)
                    run(dve, "vector", steps, expert_batch)
                    if experts is not None:
                        experts_end()
                    if last:
                        dve.wait_ge(sems["ffn_gain_loaded"], 16)
                        for t in range(TILES):
                            rows = xs[:, t * D:(t + 1) * D]
                            dve.wait_ge(sems["norm_squares"], t + 1)
                            v.tensor_scalar(st[:, 1:2], st[:, 0:1], 1.0 / D, EPS, ALU.mult, ALU.add).then_inc(
                                sems["final_var"], 1)
                            dve.wait_ge(sems["final_std"], t + 1)
                            step(v.reciprocal(st[:, 3:4], st[:, 2:3]))
                            v.scalar_tensor_tensor(out=rows, in0=rows, scalar=st[:, 3:4], in1=h_ffn[:, :],
                                                   op0=ALU.mult, op1=ALU.mult).then_inc(sems["out_ready"], 1)
                            dve.wait_ge(sems["out_ready"], t + 1)

                @block.scalar
                def _(act):
                    s = nc.scalar
                    step = Steps(act, sems["scalar_step"])

                    def expert_batch(b, half):
                        act.wait_ge(sems["u_free"], b * B + B)
                        s.activation(gelu_b[:, :], act_b[:, :], ACT.Gelu_apprx_tanh).then_inc(sems["gelu_done"], 1)
                        act.wait_ge(sems["weights_done"], b + 1)
                        for j in range(BPE):
                            act.wait_ge(sems["v_free_pe"], b * BPE + j + 1)
                            s.activation(diag[:, half * BPE + j, :], ident[:, :], ACT.Copy,
                                         scale=wgt_b[:, j:j + 1]).then_inc(sems["diag_done"], 1)

                    norms = [0]

                    def norm(src, out, squares):
                        norms[0] += 1
                        s.activation(squares, src, ACT.Square, accum_out=st[:, 0:1]).then_inc(sems["norm_squares"], 1)
                        act.wait_ge(sems["norm_var"], norms[0])
                        s.activation(st[:, 2:3], st[:, 1:2], ACT.Sqrt).then_inc(sems["norm_std"], 1)
                        act.wait_ge(sems["norm_rstd"], norms[0])
                        s.activation(out, src, ACT.Copy, scale=st[:, 3:4]).then_inc(sems["x_normed"], 1)

                    def tile_norm():
                        norm(xs[:, bass.ds(tile * D, D)], x_n, junk)

                    def copy_bank(out, job, signal=None, func=ACT.Copy, cols=None, view=None, **kw):
                        wait_filled(act, job)
                        src = bank_of(job)[:, 0:cols] if cols else bank_of(job)[:, :]
                        if view:
                            src = view(src)
                        drain(s.activation(out, src, func, **kw), job)
                        if signal:
                            wait_drained(act, job)
                            act.sem_inc(sems[signal], 1)

                    def c_t(n):
                        return lambda ap: ap.rearrange("p (c t) -> p c t", c=n)

                    def mem_kv(i):
                        if i < 4:
                            copy_bank(mem_k[:, 2 * i:2 * i + 2, :], f"MK{i}", "mem_k_ready", view=c_t(2))
                        else:
                            half = (i - 4) // 2
                            copy_bank(mem_v[:, i % 2, half * BLK:(half + 1) * BLK], f"MV{i - 4}", "mem_v_ready")

                    def rope_tables():
                        act.wait_ge(sems["rope_reduced"], 1)
                        s.activation(st[:, 24:40], st[:, 24:40], ACT.Sin).then_inc(sems["rope_sin"], 1)
                        s.activation(st[:, 8:24], st[:, 8:24], ACT.Sin).then_inc(sems["rope_sin"], 1)

                    def mem_norm():
                        act.wait_ge(sems["mem_loaded"], 16)
                        for m in range(2):
                            norm(mem_raw[:, m, :], mem_raw[:, m, :], v_rows[:, 2, :])
                        for i in range(4):
                            copy_bank(mem_t[:, (i % 2) * 4:(i % 2) * 4 + 4, (i // 2) * P:(i // 2 + 1) * P],
                                      f"MT{i}", "mem_turned", view=c_t(4))

                    def mix_norm():
                        if first:
                            act.wait_ge(sems["x_loaded"], 16)
                        tile_norm()

                    def conv_in():
                        wait_filled(act, "AB")
                        s.activation(conv_e[:, :, :], bank_of("AB")[:, 256:512].rearrange("p (g t) -> p g t", g=2),
                                     ACT.Exp, scale=-1.0).then_inc(sems["b_exp"], 1)

                    def copy_z(i):
                        if i and experts is not None:
                            act.wait_ge(sems["routed"], i)
                        copy_bank(z[:, i * BLK:(i + 1) * BLK], ("ZQ", "ZK1", "ZK2")[i], "z_copied")

                    def turn_kv():
                        copy_bank(kv_t[:, :, bass.ds(tile * P, P)], "KT", "k_turned", view=c_t(4))
                        copy_bank(q_t[:, :, :], "QT", "q_turned", view=c_t(4))
                        act.wait_ge(sems["kv_rope_done"], 1)
                        s.activation(kv_n[:, bass.ds(tile * 256, 256)].rearrange("p (k d) -> p k d", k=2),
                                     z[:, ZC["vs"]:ZC["vs"] + 512].rearrange("p (k d) -> p k d", k=2)[:, :, 0:P],
                                     ACT.Copy).then_inc(sems["v_kept"], 1)
                        copy_bank(pool_m[:, :, :], "PM", "pool_mean", cols=256, view=c_t(2))
                        s.activation(pool_prev[:, :], z[:, ZC["pool"]:ZC["pool"] + 256], ACT.Copy).then_inc(
                            sems["pool_kept"], 1)

                    def cmp_hidden():
                        wait_filled(act, "HID")
                        drain(s.activation(hid_rows[0:32, :], bank_of("HID")[0:32, :], ACT.Gelu_apprx_tanh), "HID")

                    def cmp_hidden_turn():
                        wait_filled(act, "HT")
                        hid = bank_of("HT")
                        s.activation(hid_k[:, :, :], hid[:, 0:64].rearrange("p (c n) -> p c n", c=2),
                                     ACT.Copy).then_inc(sems["cmp_hidden"], 1)
                        ins = s.activation(hid_v,
                                           hid[:, 64:128].rearrange("p (c n) -> p c n", c=4).unsqueeze(2).to_broadcast(
                                               [P, 4, HEADS, NC]), ACT.Copy)
                        drain(ins, "HT")

                    def exp_heads(scored, done, col):
                        for i in range(4):
                            act.wait_ge(sems[scored], i + 1)
                            for k in range(2):
                                h = (i % 2) * 4 + 2 * (i // 2) + k
                                s.activation(probs[:, h, :], probs[:, h, :], ACT.Exp, bias=st[:, 8 + h:9 + h],
                                             accum_out=st[:, col + h:col + h + 1]).then_inc(sems[done], 1)

                    def cmp_scores():
                        act.wait_ge(sems["cmp_max_taken"], 1)
                        s.activation(p_cmp[:, :, :], p_cmp[:, :, :], ACT.Exp).then_inc(sems["cmp_exp"], 1)

                    def turn_probs(prefix, signal):
                        for i in range(4):
                            copy_bank(probs_t[:, 2 * i:2 * i + 2, :, :].rearrange("p h c t -> p (h c) t"),
                                      f"{prefix}{i}", signal, view=c_t(4))

                    def win_turn():
                        wait_filled(act, "OS")
                        turn_probs("TW", "win_turned")

                    def conv_norm():
                        act.wait_ge(sems["conv_var"], 1)
                        s.activation(st[:, 73:74], st[:, 72:73], ACT.Sqrt).then_inc(sems["conv_std"], 1)

                    def conv_act():
                        act.wait_ge(sems["conv_affine"], 1)
                        s.activation(conv_e[:, :, :], conv[:, :, :], ACT.Exp, scale=-1.0).then_inc(sems["conv_exp"], 1)

                    def small_branches():
                        for job, lo, func, arg, by in (("PY", 6, ACT.Copy, "scale", "psc"),
                                                       ("PW", 4, ACT.Identity, "bias", "pwb")):
                            wait_filled(act, job)
                            for i in range(2):
                                ins = s.activation(cat_t[:, lo + i, :], bank_of(job)[:, i * P:(i + 1) * P], func,
                                                   **{arg: small(by, i, 1)})
                                if i == 0:
                                    step.mark(ins)
                                else:
                                    drain(ins, job)
                        step.settle()
                        for job in ("PY", "PW"):
                            wait_drained(act, job)

                    def xa_scores():
                        for i in range(2):
                            act.wait_ge(sems["xs_max"], i + 1)
                            job = f"XS{i}"
                            for k in range(2):
                                h = 2 * i + k
                                ins = s.activation(x_probs[:, h, :], bank_of(job)[:, k * N_MEM:(k + 1) * N_MEM],
                                                   ACT.Exp, bias=st[:, 16 + h:17 + h], scale=(D // XH) ** -0.5,
                                                   accum_out=st[:, 20 + h:21 + h])
                                if k == 0:
                                    ins.then_inc(sems["xs_exp"], 1)
                                else:
                                    drain(ins, job)
                                    wait_drained(act, job)
                                    act.sem_inc(sems["xs_exp"], 1)

                    def xa_turn():
                        for i in range(2):
                            copy_bank(xprobs_t[:, 2 * i:2 * i + 2, :, :].rearrange("p h c t -> p (h c) t"), f"XT{i}",
                                      "xs_turned", view=c_t(4))

                    def xa_out():
                        for i in range(2):
                            copy_bank(xo_t[:, 4 * i:4 * i + 4, :], f"XO{i}", "xo_ready", view=c_t(4))

                    def xa_norm():
                        act.wait_ge(sems["x_mixed"], 2)
                        tile_norm()

                    def ffn_norm():
                        act.wait_ge(sems["x_attended"], 2)
                        tile_norm()

                    def queries(i):
                        if i == 0:
                            act.wait_ge(sems["h_scaled"], 1)
                        copy_bank(pq_t[:, 4 * i:4 * i + 4, :], f"PQ{i}", "pq_ready", view=c_t(4))

                    def sub_scores(i):
                        copy_bank(half_s[:, 4 * i:4 * i + 4, :], f"PK{i}", "pk_ready", view=c_t(4))

                    def gate_exps(q):
                        act.wait_ge(sems["experts_ranked"], ranked(q))
                        cols = gate[:, 32 * q:32 * q + 32]
                        s.activation(cols, cols, ACT.Exp).then_inc(sems["gate_exps"], 1)

                    def start():
                        if last:
                            s.activation(junk, xs[:, 0:D], ACT.Square, accum_out=st[:, 0:1]).then_inc(
                                sems["norm_squares"], 1)

                    steps = {
                        "start": start, "rope_tables": rope_tables, "mem_norm": mem_norm, "mix_norm": mix_norm,
                        "conv_in": conv_in, "zq": lambda: copy_z(0),
                        "zk1": lambda: copy_z(1), "zk2": lambda: copy_z(2),
                        "branch_gates": lambda: copy_bank(gates[:, :], "GT", "gate_exp", func=ACT.Exp, cols=24,
                                                          scale=-1.0),
                        "turn_kv": turn_kv, "cmp_hidden": cmp_hidden,
                        "cmp_hidden_turn": cmp_hidden_turn,
                        "sel_scores": lambda: exp_heads("sel_scored", "sel_exp", 40), "cmp_scores": cmp_scores,
                        "cmp_probs": lambda: copy_bank(pt_cmp[:, :], "TCM", "cmp_turned", cols=P),
                        "sel_turn": lambda: turn_probs("TS", "sel_turned"),
                        "win_scores": lambda: exp_heads("win_scored", "win_exp", 48), "win_turn": win_turn,
                        "conv_norm": conv_norm, "conv_act": conv_act, "small_branches": small_branches,
                        "mix_turn": lambda: copy_bank(cat_t[:, 0:4, :], "OT", "cat_ready", view=c_t(4)),
                        "xa_norm": xa_norm, "xa_scores": xa_scores, "xa_turn": xa_turn, "xa_out": xa_out,
                        "ffn_norm": ffn_norm,
                    }
                    for i in range(2):
                        steps[f"xq{i}"] = lambda i=i: copy_bank(xq_t[:, 4 * i:4 * i + 4, :], f"XQ{i}", "xq_ready",
                                                                view=c_t(4))
                    for i in range(8):
                        steps[f"mem_kv{i}"] = lambda i=i: mem_kv(i)
                    for i in range(4):
                        steps[f"pq{i}"] = lambda i=i: queries(i)
                        steps[f"gates{i}"] = lambda i=i: gate_exps(i)
                        steps[f"sub_scores{i}"] = lambda i=i: sub_scores(i)
                    run(act, "scalar", steps, expert_batch)
                    if last:
                        for t in range(TILES):
                            if t == 1:
                                act.wait_ge(sems["experts_added"], 1)
                                act.wait_ge(sems["out_ready"], 1)
                                s.activation(junk, xs[:, D:2 * D], ACT.Square, accum_out=st[:, 0:1]).then_inc(
                                    sems["norm_squares"], 1)
                            act.wait_ge(sems["final_var"], t + 1)
                            s.activation(st[:, 2:3], st[:, 1:2], ACT.Sqrt).then_inc(sems["final_std"], 1)

                @block.tensor
                def _(pe):
                    def expert_batch(b, half):
                        for j in V_ORDER:
                            if j >= BPE:
                                continue
                            pe.wait_ge(v_landed[j], landed(b))
                            pe.wait_ge(sems["diag_done"], b * BPE + j + 1)
                            for c in range(2):
                                mm = pe.matmul(acc_pe[:, c * 512:(c + 1) * 512], diag[:, half * BPE + j, :],
                                               v_rows[:, j, c * 512:(c + 1) * 512], start=False, stop=False,
                                               skip_group_check=True)
                            mm.then_inc(sems["v_free_pe"], 1)

                    def open_job(job):
                        if at[job] >= BANKS:
                            pe.wait_ge(drained[at[job] % BANKS], at[job] // BANKS)
                        return bank_of(job)

                    def close_job(mm, job):
                        mm.then_inc(filled[at[job] % BANKS], 1)

                    def need_weights(name):
                        pe.wait_ge(w_landed[slot[name] % RING], 16 * (slot[name] // RING + 1))
                        return weights(name)

                    def turn(job, sources):
                        out = open_job(job)
                        for i, src in enumerate(sources):
                            mm = pe.transpose(out[:, i * P:(i + 1) * P], src, ident[:, :])
                        close_job(mm, job)

                    def product(out, pairs):
                        for i, (lhs, rhs) in enumerate(pairs):
                            mm = pe.matmul(out, lhs, rhs, start=(i == 0), stop=(i == len(pairs) - 1))
                        return mm

                    normed = [0]

                    def turn_normed(jobs2, src):
                        normed[0] += 1
                        pe.wait_ge(sems["x_normed"], normed[0])
                        for i, job in enumerate(jobs2):
                            turn(job, [src[:, (4 * i + c) * P:(4 * i + c + 1) * P] for c in range(4)])

                    def rows_product(job, w, lhs):
                        close_job(product(open_job(job)[:, :], [(lhs[:, c, :], w[:, c, :]) for c in range(KC)]), job)

                    def cols_product(job, w):
                        out = open_job(job)
                        for o in range(4):
                            mm = product(out[:, o * P:(o + 1) * P],
                                         [(w[:, c, o * P:(o + 1) * P], h_t[:, c, :]) for c in range(KC)])
                        close_job(mm, job)

                    def mem_norm():
                        for m in range(2):
                            turn_normed([f"MT{2 * m}", f"MT{2 * m + 1}"], mem_raw[:, m, :])

                    def mem_kv(i):
                        pe.wait_ge(sems["mem_gained"], 1)
                        w = need_weights(MEM_BLOCKS[i // 2])
                        k = i % 2
                        if i < 4:
                            job = f"MK{i}"
                            out = open_job(job)
                            for n in range(2):
                                o = 2 * k + n
                                mm = product(out[:, n * N_MEM:(n + 1) * N_MEM],
                                             [(w[:, c, o * P:(o + 1) * P], mem_g[:, c, :]) for c in range(KC)])
                        else:
                            job = f"MV{i - 4}"
                            mm = product(open_job(job)[:, :],
                                         [(mem_g[:, c, k * P:(k + 1) * P], w[:, c, :]) for c in range(KC)])
                        close_job(mm, job)

                    def tile_turned(jobs2):
                        turn_normed(jobs2, x_n)
                        for job in jobs2:
                            wait_drained(pe, job)

                    def mix_norm():
                        if first:
                            pe.wait_ge(sems["ident_loaded"], 16)
                        tile_turned(["NT0", "NT1"])

                    def gate_products():
                        wg = small("wg").rearrange("p (c n) -> p c n", c=KC)
                        pe.wait_ge(sems["smalls_loaded"], 16)
                        close_job(product(open_job("GT")[:, 0:24], [(h_t[:, c, :], wg[:, c, :]) for c in range(KC)]),
                                  "GT")

                    def turn_kv():
                        pe.wait_ge(sems["kv_rope_done"], 1)
                        turn("KT", [z[:, ZC[n]:ZC[n] + P] for n in ("kc", "vc", "ks", "kw")])
                        turn("QT", [z[:, i * P:(i + 1) * P] for i in range(4)])
                        out = open_job("PM")
                        pe.wait_ge(sems["tile_consts_loaded"], 16)
                        for g in range(4):
                            dst = out[(g % 2) * 64:(g % 2) * 64 + 64, (g // 2) * P:(g // 2 + 1) * P]
                            mm = product(dst, [
                                (z[:, ZC["pool"] + g * 64:ZC["pool"] + g * 64 + 64], tile_const("cur", g * P, P)),
                                (pool_prev[:, g * 64:g * 64 + 64], tile_const("prev", g * P, P))])
                        close_job(mm, "PM")

                    def cmp_hidden():
                        pe.wait_ge(sems["cmp_in_built"], 16)
                        out = open_job("HID")
                        for kind, name in enumerate(("ck", "cv")):
                            w = need_weights(name).rearrange("p c n -> p (c n)").rearrange("p (c n) -> p c n", c=16)
                            mm = product(out[0:32, kind * 256:(kind + 1) * 256],
                                         [(cmp_in[:, kind, c, :], w[:, c, :]) for c in range(16)])
                        close_job(mm, "HID")

                    def cmp_hidden_turn():
                        wait_drained(pe, "HID")
                        out = open_job("HT")
                        for i in range(4):
                            mm = pe.transpose(out[:, i * 32:(i + 1) * 32], hid_rows[0:32, i * P:(i + 1) * P],
                                              ident[0:32, 0:32])
                        close_job(mm, "HT")

                    def cmp_kv():
                        pe.wait_ge(sems["cmp_hidden"], 1)
                        wait_drained(pe, "HT")
                        out = open_job("KC")
                        w2 = small("w2").rearrange("p (k c d) -> p k c d", k=2, c=2)
                        for kvh in range(KV_HEADS):
                            product(out[kvh * HD:(kvh + 1) * HD, 0:NC],
                                    [(w2[:, 0, c, :], hid_k[:, c, kvh * NC:(kvh + 1) * NC]) for c in range(2)])
                        for kvh in range(KV_HEADS):
                            mm = product(out[:, NC + kvh * HD:NC + (kvh + 1) * HD],
                                         [(hid_v[:, 2 * c + kvh, :, :].rearrange("p h n -> p (h n)"), w2[:, 1, c, :])
                                          for c in range(2)])
                        close_job(mm, "KC")

                    def head_rows(h):
                        return slice((h // 4) * HD, (h // 4 + 1) * HD)

                    def scores(prefix, kind):
                        pe.wait_ge(sems["q_turned"], 1)
                        pe.wait_ge(sems["k_turned"], 1)
                        for i in range(4):
                            out = open_job(f"{prefix}{i}")
                            for k in range(2):
                                h = (i % 2) * 4 + 2 * (i // 2) + k
                                mm = product(out[:, k * S:(k + 1) * S],
                                             [(q_t[head_rows(h), h % 4, :], kv_t[head_rows(h), kind, 0:S])])
                            close_job(mm, f"{prefix}{i}")

                    def cmp_scores():
                        wait_drained(pe, "KC")
                        for i in range(2):
                            out = open_job(f"SC{i}")
                            for k in range(4):
                                h = 4 * i + k
                                mm = product(out[:, k * NC:(k + 1) * NC],
                                             [(q_t[head_rows(h), k, :], cmp_kt[head_rows(h), :])])
                            close_job(mm, f"SC{i}")

                    def turn_probs(prefix, done):
                        order = [(i % 2) * 4 + 2 * (i // 2) + k for i in range(4) for k in range(2)]
                        for i in range(4):
                            h = [2 * i, 2 * i + 1]
                            pe.wait_ge(sems[done], max(order.index(n) for n in h) + 1)
                            turn(f"{prefix}{i}", [probs[:, n, c * P:(c + 1) * P] for n in h for c in range(2)])

                    def weighted(job, kind, turned):
                        pe.wait_ge(sems[turned], 4)
                        pe.wait_ge(sems["v_kept"], 1)
                        out = open_job(job)
                        for h in range(HEADS):
                            cols = kind * P + (h // 4) * HD
                            mm = product(out[:, h * HD:(h + 1) * HD],
                                         [(probs_t[:, h, c, :], kv_n[:, c * 256 + cols:c * 256 + cols + HD])
                                          for c in range(2)])
                        close_job(mm, job)

                    def cmp_probs():
                        pe.wait_ge(sems["cmp_probs_ready"], 1)
                        turn("TCM", [p_cmp[:, :, :].rearrange("p h n -> p (h n)")])

                    def cmp_out():
                        pe.wait_ge(sems["cmp_turned"], 1)
                        close_job(product(open_job("OC")[:, :],
                                          [(pt_cmp[:, :], cmp_vb[:, :, :].rearrange("p h d -> p (h d)"))]), "OC")

                    def conv_norm():
                        pe.wait_ge(sems["conv_out"], 1)
                        turn("CT", [conv[:, g, :] for g in range(2)])

                    def conv_act():
                        wait_drained(pe, "CT")
                        turn("CB", [conv_u[:, g, :] for g in range(2)])

                    def small_branches():
                        pe.wait_ge(sems["pool_mean"], 1)
                        out = open_job("PY")
                        pbd = small("pbd").rearrange("p (k n) -> p k n", k=2)
                        for i in range(2):
                            mm = product(out[:, i * P:(i + 1) * P], [(pbd[:, i, :], pool_m[:, i, :])])
                        close_job(mm, "PY")
                        pe.wait_ge(sems["conv_silu"], 1)
                        out = open_job("PW")
                        pw = small("pw").rearrange("p (c n) -> p c n", c=2)
                        for o in range(2):
                            mm = product(out[:, o * P:(o + 1) * P],
                                         [(pw[:, c, o * P:(o + 1) * P], conv_u[:, c, :]) for c in range(2)])
                        close_job(mm, "PW")

                    def mix_turn():
                        pe.wait_ge(sems["o_mixed"], 1)
                        turn("OT", [o_sum[:, c * P:(c + 1) * P] for c in range(4)])

                    def wo(i):
                        pe.wait_ge(sems["cat_ready"], 1)
                        rows_product(f"WO{i}", need_weights(f"wo{i}"), cat_t)

                    def xa_scores():
                        pe.wait_ge(sems["xq_ready"], 2)
                        if first:
                            pe.wait_ge(sems["mem_k_ready"], 4)
                        for i in range(2):
                            out = open_job(f"XS{i}")
                            for k in range(2):
                                h = 2 * i + k
                                mm = product(out[:, k * N_MEM:(k + 1) * N_MEM],
                                             [(xq_t[:, 2 * h + c, :], mem_k[:, 2 * h + c, :]) for c in range(2)])
                            close_job(mm, f"XS{i}")

                    def xa_turn():
                        pe.wait_ge(sems["xs_probs"], 1)
                        for i in range(2):
                            turn(f"XT{i}", [x_probs[:, h, c * P:(c + 1) * P] for h in (2 * i, 2 * i + 1)
                                            for c in range(2)])

                    def xa_out():
                        pe.wait_ge(sems["xs_turned"], 2)
                        if first:
                            pe.wait_ge(sems["mem_v_ready"], 4)
                        for i in range(2):
                            out = open_job(f"XO{i}")
                            for k in range(4):
                                o = 4 * i + k
                                mm = product(out[:, k * P:(k + 1) * P],
                                             [(mem_v[:, m, o * P:(o + 1) * P], xprobs_t[:, o // 2, m, :])
                                              for m in range(2)])
                            close_job(mm, f"XO{i}")

                    def xo(i):
                        pe.wait_ge(sems["xo_ready"], 2)
                        rows_product(f"XW{i}", need_weights(f"xo{i}"), xo_t)

                    def sub_scores(i):
                        subk = small("subk").rearrange("p (e n) -> p e n", e=2)
                        pe.wait_ge(sems["pq_ready"], i + 1)
                        out = open_job(f"PK{i}")
                        for k in range(4):
                            j = 4 * i + k
                            mm = product(out[:, k * P:(k + 1) * P], [(pq_t[:, j, :], subk[:, j % 2, :])])
                        close_job(mm, f"PK{i}")

                    def start():
                        if experts is not None:
                            for _ in range(2 * BPE):
                                pe.sem_inc(sems["v_free_pe"], 1)
                            for c in range(2):
                                pe.matmul(acc_pe[:, c * 512:(c + 1) * 512], zero[:, :], xs[:, 0:512], start=True,
                                          stop=False, skip_group_check=True)

                    steps = {
                        "start": start, "mem_norm": mem_norm, "mix_norm": mix_norm,
                        "ab": lambda: cols_product("AB", need_weights("ab")),
                        "zq": lambda: rows_product("ZQ", need_weights("zq"), h_t),
                        "zk1": lambda: rows_product("ZK1", need_weights("zk1"), h_t),
                        "zk2": lambda: rows_product("ZK2", need_weights("zk2"), h_t),
                        "branch_gates": gate_products, "turn_kv": turn_kv, "cmp_hidden": cmp_hidden,
                        "cmp_hidden_turn": cmp_hidden_turn,
                        "sel_scores": lambda: scores("SS", 2), "cmp_kv": cmp_kv, "cmp_scores": cmp_scores,
                        "cmp_probs": cmp_probs, "sel_turn": lambda: turn_probs("TS", "sel_exp"), "cmp_out": cmp_out,
                        "sel_out": lambda: weighted("OS", 0, "sel_turned"), "win_scores": lambda: scores("SW", 3),
                        "win_turn": lambda: turn_probs("TW", "win_exp"),
                        "win_out": lambda: weighted("OW", 1, "win_turned"), "conv_norm": conv_norm,
                        "conv_act": conv_act, "small_branches": small_branches, "mix_turn": mix_turn,
                        "xa_norm": lambda: tile_turned(["NX0", "NX1"]), "xa_scores": xa_scores, "xa_turn": xa_turn,
                        "xa_out": xa_out, "ffn_norm": lambda: tile_turned(["NF0", "NF1"]),
                    }
                    for i in range(2):
                        steps[f"wo{i}"] = lambda i=i: wo(i)
                        steps[f"xq{i}"] = lambda i=i: cols_product(f"XQ{i}", need_weights(f"xq{i}"))
                        steps[f"xo{i}"] = lambda i=i: xo(i)
                    for i in range(8):
                        steps[f"mem_kv{i}"] = lambda i=i: mem_kv(i)
                    for i in range(4):
                        steps[f"pq{i}"] = lambda i=i: cols_product(f"PQ{i}", need_weights(f"pq{i}"))
                        steps[f"sub_scores{i}"] = lambda i=i: sub_scores(i)
                    run(pe, "tensor", steps, expert_batch)

            nc.gpsimd.sem_clear(range(stage_sems[0], stage_sems[-1] + 1))
            nc.all_engine_barrier(sem_only=True)

        pool_m = sb("pool_m", [P, 2, P])
        stage(0, None, mem_layer=0, first=True)
        stage(1, 0, mem_layer=1)
        with nc.Fori(1, STAGES - 1) as s:
            stage(s + 1, s)
        stage(None, STAGES - 1, last=True)


def columns(w):
    return w.reshape(-1, P, w.shape[-1]).transpose(1, 0, 2)


def constants():
    t = np.arange(P)
    tile_consts = np.zeros((TILES, P, N_TC), np.float32)

    def put(tile, name, value):
        at, w = TC[name]
        tile_consts[tile, :, at:at + w] = value

    for tile in range(TILES):
        tok = tile * P + t
        put(tile, "causal", np.where(np.arange(S)[None, :] <= tok[:, None], 0.0, NEG))
        n = np.arange(NC)
        ok = (n[None, :] * CMP_STRIDE + CMP_BLOCK - 1 <= tok[:, None]) & (n[None, :] < N_CMP)
        put(tile, "cadd", np.where(ok, 0.0, NEG))
        put(tile, "cvalid", ok)
        cur, prev = np.zeros((P, 4, P)), np.zeros((P, 4, P))
        for g, w in enumerate(POOL_WINDOWS):
            start = np.maximum(tok + 1 - w, 0)
            for o in range(P):
                for i in range(start[o], tok[o] + 1):
                    which = cur if i >= tile * P else prev
                    which[i % P, g, o] = np.float32(1.0 / (tok[o] + 1 - start[o])) - (1.0 if i == tok[o] else 0.0)
        put(tile, "cur", cur.reshape(P, -1))
        put(tile, "prev", prev.reshape(P, -1))
        put(tile, "flag", float(tile > 0))
    head_mask = (t[:, None] // NC == np.arange(HEADS)[None, :]).astype(np.float32)
    freqs = np.float32(THETA) ** (-np.arange(HALF, dtype=np.float32) * np.float32(2.0) / np.float32(ROT))
    return tile_consts, head_mask, freqs.astype(np.float32)


def kernel(**inputs):
    import concourse.bacc as _bacc
    from concourse.bass_utils import run_bass_kernel_spmd as _run

    given = {n: np.asarray(v) for n, v in inputs.items()}
    tile_consts, head_mask, freqs = constants()

    blocks = np.zeros((DEPTH * len(WHERE), P, KC * BLK), np.float32)
    smalls = np.zeros((DEPTH, P, N_SMALL), np.float32)
    for l in range(DEPTH):
        def put_block(name, w):
            blocks[l * len(WHERE) + WHERE[name]] = columns(w).reshape(P, -1)

        def put(name, value):
            at, w = SMALL[name]
            smalls[l, :, at:at + w] = np.asarray(value).reshape(P, w)

        w_in = given["w_in"][l]
        put_block("zq", w_in[:, 0:512].reshape(D, KV_HEADS, 4, HD).transpose(0, 2, 1, 3).reshape(D, 512))
        put_block("zk1", w_in[:, 512:1024])
        put_block("zk2", np.concatenate([w_in[:, 1024:1280], w_in[:, 1816:2072]], 1))
        put_block("ab", w_in[:, 1304:1816])
        put_block("ck", given["cmp_w1"][l, 0])
        put_block("cv", given["cmp_w1"][l, 1])
        for name, w, n in (("wo", given["w_out"][l], 2), ("xq", given["xa_wq"][l], 2), ("xo", given["xa_wo"][l], 2),
                           ("pq", given["peer_wq"][l], 4), ("mk", given["xa_wkv"][l][:, 0:D], 2),
                           ("mv", given["xa_wkv"][l][:, D:2 * D], 2)):
            for i in range(n):
                put_block(f"{name}{i}", w[:, i * BLK:(i + 1) * BLK])
        put("w2", given["cmp_w2"][l].reshape(2, 2, P, HD).transpose(2, 0, 1, 3))
        pe = given["cmp_pe"][l].reshape(2, 16, 2, HD).transpose(3, 0, 2, 1)
        put("pe", np.concatenate([pe, pe], 0))
        put("cw", given["conv_w"][l].reshape(CONV_W, 2, P).transpose(2, 1, 0))
        for name, key in (("cb", "conv_b"), ("lng", "conv_ln_g"), ("lnb", "conv_ln_b"), ("pwb", "conv_pw_b"),
                          ("psc", "pool_scale"), ("gmix", "norm_mix_g"), ("gxa", "norm_xa_g"), ("gffn", "norm_ffn_g")):
            put(name, given[key][l].reshape(-1, P).T)
        put("pw", columns(given["conv_pw_w"][l]))
        pbd = np.zeros((2, 2, 64, 2, 64), np.float32)
        for g in range(4):
            pbd[g // 2, g % 2, :, g % 2, :] = given["pool_w"][l, g]
        put("pbd", pbd.reshape(2, P, P).transpose(1, 0, 2))
        put("wg", columns(w_in[:, 1280:1304]))
        put("subk", given["peer_subkeys"][l].transpose(2, 0, 1))
        put("first", np.full((P, 1), l * EXPERTS))
    fixed = np.concatenate([
        head_mask, np.tile(np.arange(TOPK, dtype=np.float32), (P, 1)), np.tile(freqs, (P, 1)),
        given["norm_mem_g"].reshape(DEPTH, KC, P).transpose(2, 0, 1).reshape(P, DEPTH * KC)], 1)

    arrays = {
        "x": given["x"].reshape(TILES, P, D).transpose(1, 0, 2),
        "mem": given["mem"].reshape(2, P, D).transpose(1, 0, 2),
        "positions": given["positions"].reshape(TILES, P).T,
        "blocks": blocks, "smalls": smalls, "tile_consts": tile_consts,
        "ident": np.eye(P, dtype=np.float32), "fixed": fixed,
        "ffn_gain": np.tile(given["norm_ffn_g"][:, None, :], (1, P, 1)),
        "final_gain": np.tile(given["final_g"][None, :], (P, 1)),
        "u": given["peer_u"].reshape(DEPTH * EXPERTS, D), "v": given["peer_v"].reshape(DEPTH * EXPERTS, D),
    }
    nc = _bacc.Bacc("TRN2", target_bir_lowering=False, num_devices=1)
    args, sent = {}, {}
    for name, value in arrays.items():
        value = np.ascontiguousarray(value)
        sent[f"{name}_in"] = value
        args[name] = nc.dram_tensor(f"{name}_in", value.shape, mybir.dt.from_np(value.dtype),
                                    kind="ExternalInput").ap()
    args["out"] = nc.dram_tensor("hidden_out", (S, D), F32, kind="ExternalOutput").ap()
    build_program(nc, args)
    result = _run(nc, [sent], core_ids=[0])
    return result.results[0]["hidden_out"].reshape(1, S, D)
```
